# Optimizing a Trainium2 kernel written in Bass

```python
import jax
import jax.numpy as jnp
from jax import lax
import numpy as np
import jax, jax.numpy as jnp

D_MODEL = 2048
BATCH = 1
SEQ = 256
DEPTH = 1

D_MIX = D_MODEL
D_RWKV = D_MIX // 2
RWKV_HEAD = 64
RWKV_HEADS = D_RWKV // RWKV_HEAD
D_POOL = D_MIX - D_RWKV
POOL_WINDOWS = (2, 4, 8, 16)
N_POOL_GROUPS = len(POOL_WINDOWS)
POOL_GROUP = D_POOL // N_POOL_GROUPS
DECAY_LORA = max(32, int(round(1.8 * D_RWKV ** 0.5 / 32)) * 32)
AAA_LORA = max(32, int(round(1.8 * D_RWKV ** 0.5 / 32)) * 32)
GATE_LORA = max(32, int(round(0.6 * D_RWKV ** 0.8 / 32)) * 32)
RWKV_SPLITS = (D_RWKV, 2 * D_RWKV, 3 * D_RWKV, 3 * D_RWKV + DECAY_LORA, 3 * D_RWKV + DECAY_LORA + AAA_LORA)
N_RWKV_COLS = 3 * D_RWKV + DECAY_LORA + AAA_LORA + GATE_LORA
D_IN = N_RWKV_COLS + D_POOL
D_FF = ((8 * D_MODEL // 3 + 255) // 256) * 256
CONV_WIDTH = 3
N_MOD = 6
RMS_EPS = 1e-6
GN_EPS = 64e-5
L2_EPS = 1e-12


def _rmsnorm(x, g):
    xf = x.astype(jnp.float32)
    y = xf * lax.rsqrt(jnp.mean(xf * xf, axis=-1, keepdims=True) + RMS_EPS)
    return (y * g.astype(jnp.float32)).astype(x.dtype)

def _token_shift(z):
    return jnp.pad(z, ((0, 0), (1, 0), (0, 0)))[:, :-1]

def _wkv7_scan(r, w, k, v, a, b):
    B, T, H, N = r.shape

    def step(S, inp):
        r_t, w_t, k_t, v_t, a_t, b_t = inp
        sa = jnp.einsum('bhvk,bhk->bhv', S, a_t)
        S = S * w_t[:, :, None, :] + sa[..., None] * b_t[:, :, None, :] + v_t[..., None] * k_t[:, :, None, :]
        y = jnp.einsum('bhvk,bhk->bhv', S, r_t)
        return S, y

    xs = (jnp.moveaxis(r, 1, 0), jnp.moveaxis(w, 1, 0), jnp.moveaxis(k, 1, 0),
          jnp.moveaxis(v, 1, 0), jnp.moveaxis(a, 1, 0), jnp.moveaxis(b, 1, 0))
    S0 = jnp.zeros((B, H, N, N), jnp.float32)
    _, ys = lax.scan(step, S0, xs)
    return jnp.moveaxis(ys, 0, 1)

def _rwkv7_mixer(p, mu, w0, w2, a0, a2, g2, k_k, k_a, r_k, ln_w, ln_b):
    B, T, _ = p.shape
    f32 = jnp.float32
    p = p + mu * (_token_shift(p) - p)
    r, k, v, xw, xa, xg = jnp.split(p, list(RWKV_SPLITS), axis=-1)
    w = -jax.nn.softplus(-(w0 + jnp.tanh(xw) @ w2)) - 0.5
    a = jax.nn.sigmoid(a0 + xa @ a2)
    g = jax.nn.sigmoid(xg) @ g2

    def heads(z):
        return z.reshape(B, T, RWKV_HEADS, RWKV_HEAD)

    kk = heads(k * k_k).astype(f32)
    kk = kk / jnp.maximum(jnp.sqrt(jnp.sum(kk * kk, axis=-1, keepdims=True)), L2_EPS)
    k = k * (1.0 + (a - 1.0) * k_a)
    r_h, k_h, v_h, a_h = heads(r), heads(k), heads(v), heads(a)
    decay = jnp.exp(-jnp.exp(heads(w).astype(f32)))
    y = _wkv7_scan(r_h.astype(f32), decay, k_h.astype(f32), v_h.astype(f32),
                   -kk, kk * a_h.astype(f32))
    mean = jnp.mean(y, axis=-1, keepdims=True)
    var = jnp.mean(jnp.square(y - mean), axis=-1, keepdims=True)
    y = ((y - mean) * lax.rsqrt(var + GN_EPS)).reshape(B, T, D_RWKV)
    y = (y * ln_w.astype(f32) + ln_b.astype(f32)).astype(p.dtype)
    bonus = jnp.sum(r_h * k_h * r_k, axis=-1, keepdims=True) * v_h
    return (y + bonus.reshape(B, T, D_RWKV)) * g

def _pool_mixer(u, pool_w, pool_b, pool_scale):
    B, T, _ = u.shape
    uf = u.astype(jnp.float32).reshape(B, T, N_POOL_GROUPS, POOL_GROUP)
    cs = jnp.cumsum(uf, axis=1)
    pos = jnp.arange(1, T + 1, dtype=jnp.float32)
    outs = []
    for gi, win in enumerate(POOL_WINDOWS):
        c_g = cs[:, :, gi]
        lag = jnp.pad(c_g, ((0, 0), (win, 0), (0, 0)))[:, :T]
        mean = (c_g - lag) / jnp.minimum(pos, win)[None, :, None]
        outs.append(mean - uf[:, :, gi])
    z = jnp.stack(outs, axis=2).astype(u.dtype)
    z = jnp.einsum('btgc,gcd->btgd', z, pool_w) + pool_b
    return z.reshape(B, T, D_POOL) * pool_scale

def _conv_ffn(h, w_up, conv_w, conv_b, w_down):
    T = h.shape[1]
    u = h @ w_up
    up = jnp.pad(u, ((0, 0), (CONV_WIDTH - 1, 0), (0, 0)))
    y = conv_b
    for j in range(CONV_WIDTH):
        y = y + conv_w[j] * up[:, j:j + T]
    val, gate = jnp.split(y, 2, axis=-1)
    return (jax.nn.silu(gate) * val) @ w_down

def first_inputs(seed: int = 0) -> dict:
    key = jax.random.key(seed)
    ks = jax.random.split(key, 27)
    L = DEPTH

    def nrm(k, shape, scale):
        return jax.random.normal(k, shape, jnp.float32) * scale

    ratio = jnp.arange(D_RWKV, dtype=jnp.float32) / (D_RWKV - 1)
    w0 = (-7.0 + 5.0 * ratio ** 0.85 + 0.5)[None, :] + nrm(ks[5], (L, D_RWKV), 0.1)
    return {
        'x': nrm(ks[0], (BATCH, SEQ, D_MODEL), 1.0),
        'c': nrm(ks[1], (BATCH, D_MODEL), 1.0),
        'w_ada': nrm(ks[2], (L, D_MODEL, N_MOD * D_MODEL), D_MODEL ** -0.5),
        'b_ada': nrm(ks[3], (L, N_MOD * D_MODEL), 0.01),
        'norm1_g': 1.0 + nrm(ks[4], (L, D_MODEL), 0.05),
        'w_in': nrm(ks[6], (L, D_MODEL, D_IN), D_MODEL ** -0.5),
        'mu_shift': jax.random.uniform(ks[7], (L, N_RWKV_COLS), jnp.float32),
        'w0': w0,
        'w2': nrm(ks[8], (L, DECAY_LORA, D_RWKV), 0.5 * DECAY_LORA ** -0.5),
        'a0': nrm(ks[9], (L, D_RWKV), 0.1),
        'a2': nrm(ks[10], (L, AAA_LORA, D_RWKV), AAA_LORA ** -0.5),
        'g2': nrm(ks[11], (L, GATE_LORA, D_RWKV), GATE_LORA ** -0.5),
        'k_k': 0.85 + nrm(ks[12], (L, D_RWKV), 0.05),
        'k_a': 1.0 + nrm(ks[13], (L, D_RWKV), 0.05),
        'r_k': nrm(ks[14], (L, RWKV_HEADS, RWKV_HEAD), 0.1),
        'ln_x_w': 1.0 + nrm(ks[15], (L, D_RWKV), 0.05),
        'ln_x_b': nrm(ks[16], (L, D_RWKV), 0.01),
        'pool_w': nrm(ks[17], (L, N_POOL_GROUPS, POOL_GROUP, POOL_GROUP), POOL_GROUP ** -0.5),
        'pool_b': nrm(ks[18], (L, N_POOL_GROUPS, POOL_GROUP), 0.01),
        'pool_scale': 1.0 + nrm(ks[19], (L, D_POOL), 0.05),
        'w_out': nrm(ks[20], (L, D_MIX, D_MODEL), D_MIX ** -0.5),
        'norm2_g': 1.0 + nrm(ks[21], (L, D_MODEL), 0.05),
        'w_up': nrm(ks[22], (L, D_MODEL, 2 * D_FF), D_MODEL ** -0.5),
        'conv_w': nrm(ks[23], (L, CONV_WIDTH, 2 * D_FF), CONV_WIDTH ** -0.5),
        'conv_b': nrm(ks[24], (L, 2 * D_FF), 0.01),
        'w_down': nrm(ks[25], (L, D_FF, D_MODEL), D_FF ** -0.5),
        'norm_f_g': 1.0 + nrm(ks[26], (D_MODEL,), 0.05),
    }

def first_block(x, c, w_ada, b_ada, norm1_g, w_in, mu_shift, w0, w2, a0, a2, g2,
              k_k, k_a, r_k, ln_x_w, ln_x_b, pool_w, pool_b, pool_scale, w_out,
              norm2_g, w_up, conv_w, conv_b, w_down, norm_f_g):
    c_act = jax.nn.silu(c)
    for l in range(DEPTH):
        mod = c_act @ w_ada[l] + b_ada[l]
        sh1, sc1, gt1, sh2, sc2, gt2 = jnp.split(mod[:, None, :], N_MOD, axis=-1)
        h = _rmsnorm(x, norm1_g[l]) * (1.0 + sc1) + sh1
        p = h @ w_in[l]
        y_rwkv = _rwkv7_mixer(p[..., :N_RWKV_COLS], mu_shift[l], w0[l], w2[l], a0[l], a2[l],
                              g2[l], k_k[l], k_a[l], r_k[l], ln_x_w[l], ln_x_b[l])
        y_pool = _pool_mixer(p[..., N_RWKV_COLS:], pool_w[l], pool_b[l], pool_scale[l])
        mix = jnp.concatenate([y_rwkv, y_pool], axis=-1) @ w_out[l]
        x = x + gt1 * mix
        h = _rmsnorm(x, norm2_g[l]) * (1.0 + sc2) + sh2
        x = x + gt2 * _conv_ffn(h, w_up[l], conv_w[l], conv_b[l], w_down[l])
    return _rmsnorm(x, norm_f_g)


D_CONV = D_MODEL // 2
N_HEADS = 16
N_KV_HEADS = 4
HEAD_DIM = 64
D_ATTN = N_HEADS * HEAD_DIM
D_KV = N_KV_HEADS * HEAD_DIM
WINDOW = 128
BLOCK = 128
ROPE_THETA = 10000.0
N_BRANCH = 2
D_FF_2 = 5632
EPS = 1e-6

SPLIT_SIZES = (D_CONV, D_CONV, D_CONV, D_ATTN, D_KV, D_KV, D_MODEL, D_MODEL)
SPLIT_POINTS = tuple(int(p) for p in np.cumsum(SPLIT_SIZES)[:-1])
D_IN_PROJ = int(sum(SPLIT_SIZES))


def rmsnorm(x, g):
    xf = x.astype(jnp.float32)
    y = xf * lax.rsqrt(jnp.mean(xf * xf, axis=-1, keepdims=True) + EPS)
    return (y * g.astype(jnp.float32)).astype(x.dtype)

def centred_dwconv3(x, w):
    xp = jnp.pad(x, ((0, 0), (1, 1), (0, 0)))
    return xp[:, :-2] * w[0] + xp[:, 1:-1] * w[1] + xp[:, 2:] * w[2]

def rope(x, seq_len):
    half = HEAD_DIM // 2
    inv_freq = ROPE_THETA ** (-jnp.arange(0, half, dtype=jnp.float32) / half)
    ang = jnp.arange(seq_len, dtype=jnp.float32)[:, None] * inv_freq[None, :]
    cos = jnp.cos(ang)[None, :, None, :]
    sin = jnp.sin(ang)[None, :, None, :]
    xf = x.astype(jnp.float32)
    x1, x2 = xf[..., :half], xf[..., half:]
    out = jnp.concatenate([x1 * cos - x2 * sin, x2 * cos + x1 * sin], axis=-1)
    return out.astype(x.dtype)

def banded_window_attention(q, k, v, sink):
    b, s = q.shape[0], q.shape[1]
    nb = s // BLOCK
    grp = N_HEADS // N_KV_HEADS
    qb = q.reshape(b, nb, BLOCK, N_KV_HEADS, grp, HEAD_DIM)
    pad = ((0, 0), (BLOCK, BLOCK), (0, 0), (0, 0))
    kp = jnp.pad(k, pad).reshape(b, nb + 2, BLOCK, N_KV_HEADS, HEAD_DIM)
    vp = jnp.pad(v, pad).reshape(b, nb + 2, BLOCK, N_KV_HEADS, HEAD_DIM)
    kb = jnp.concatenate([kp[:, :-2], kp[:, 1:-1], kp[:, 2:]], axis=2)
    vb = jnp.concatenate([vp[:, :-2], vp[:, 1:-1], vp[:, 2:]], axis=2)
    scale = HEAD_DIM ** -0.5
    scores = jnp.einsum('bnqkgd,bnskd->bnkgqs', qb, kb).astype(jnp.float32) * scale
    blk = jnp.arange(nb)[:, None, None]
    qpos = blk * BLOCK + jnp.arange(BLOCK)[None, :, None]
    kpos = (blk - 1) * BLOCK + jnp.arange(3 * BLOCK)[None, None, :]
    mask = (jnp.abs(kpos - qpos) <= WINDOW) & (kpos >= 0) & (kpos < s)
    scores = jnp.where(mask[None, :, None, None], scores, -jnp.inf)
    sk = sink.astype(jnp.float32).reshape(1, 1, N_KV_HEADS, grp, 1)
    m = jnp.maximum(jnp.max(scores, axis=-1), sk)
    p = jnp.exp(scores - m[..., None])
    denom = jnp.sum(p, axis=-1) + jnp.exp(sk - m)
    p = (p / denom[..., None]).astype(v.dtype)
    out = jnp.einsum('bnkgqs,bnskd->bnqkgd', p, vb)
    return out.reshape(b, s, N_HEADS, HEAD_DIM)

def second_inputs(seed: int = 0) -> dict:
    key = jax.random.key(seed)
    ks = jax.random.split(key, 16)
    f32 = jnp.float32

    def nrm(k, shape, fan_in):
        return jax.random.normal(k, shape, f32) * (fan_in ** -0.5)

    x = jax.random.normal(ks[0], (BATCH, SEQ, D_MODEL), f32)
    return {
        "x": x,
        "norm_mix_g": 1.0 + 0.02 * jax.random.normal(ks[1], (DEPTH, D_MODEL), f32),
        "w_in": nrm(ks[2], (DEPTH, D_MODEL, D_IN_PROJ), D_MODEL),
        "b_gate": 0.02 * jax.random.normal(ks[3], (DEPTH, N_BRANCH * D_MODEL), f32),
        "conv_a_w": nrm(ks[4], (DEPTH, CONV_WIDTH, D_CONV), CONV_WIDTH),
        "w_out_a": nrm(ks[5], (DEPTH, D_CONV, D_MODEL), D_CONV),
        "sink_logits": 0.5 * jax.random.normal(ks[6], (DEPTH, N_HEADS), f32),
        "w_o_attn": nrm(ks[7], (DEPTH, D_ATTN, D_MODEL), D_ATTN),
        "w_mix_out": nrm(ks[8], (DEPTH, D_MODEL, D_MODEL), D_MODEL),
        "norm_ffn_g": 1.0 + 0.02 * jax.random.normal(ks[9], (DEPTH, D_MODEL), f32),
        "ffn_w_up": nrm(ks[10], (DEPTH, D_MODEL, 2 * D_FF_2), D_MODEL),
        "ffn_conv_w": nrm(ks[11], (DEPTH, CONV_WIDTH, 2 * D_FF_2), CONV_WIDTH),
        "ffn_conv_b": 0.02 * jax.random.normal(ks[12], (DEPTH, 2 * D_FF_2), f32),
        "ffn_w_down": nrm(ks[13], (DEPTH, D_FF_2, D_MODEL), D_FF_2),
        "norm_final_g": 1.0 + 0.02 * jax.random.normal(ks[14], (D_MODEL,), f32),
    }

def second_block(x, norm_mix_g, w_in, b_gate, conv_a_w, w_out_a, sink_logits, w_o_attn,
              w_mix_out, norm_ffn_g, ffn_w_up, ffn_conv_w, ffn_conv_b, ffn_w_down,
              norm_final_g):
    b, s, _ = x.shape
    h = x
    for l in range(DEPTH):
        u = rmsnorm(h, norm_mix_g[l])
        z = u @ w_in[l]
        b_a, c_a, v_a, q, k, v, gl_a, gl_b = jnp.split(z, SPLIT_POINTS, axis=-1)
        y_a = (b_a * centred_dwconv3(c_a * v_a, conv_a_w[l])) @ w_out_a[l]
        q = rope(q.reshape(b, s, N_HEADS, HEAD_DIM), s)
        k = rope(k.reshape(b, s, N_KV_HEADS, HEAD_DIM), s)
        v = v.reshape(b, s, N_KV_HEADS, HEAD_DIM)
        att = banded_window_attention(q, k, v, sink_logits[l])
        y_b = att.reshape(b, s, D_ATTN) @ w_o_attn[l]
        g_a = jax.nn.sigmoid(gl_a + b_gate[l, :D_MODEL])
        g_b = jax.nn.sigmoid(gl_b + b_gate[l, D_MODEL:])
        h = h + (g_a * y_a + g_b * y_b) @ w_mix_out[l]
        u2 = rmsnorm(h, norm_ffn_g[l])
        up = centred_dwconv3(u2 @ ffn_w_up[l], ffn_conv_w[l]) + ffn_conv_b[l]
        a, gv = up[..., :D_FF_2], up[..., D_FF_2:]
        h = h + (jax.nn.silu(a) * gv) @ ffn_w_down[l]
    return rmsnorm(h, norm_final_g)


def setup_inputs(seed=0):
    out = dict(first_inputs(seed))
    for name, value in second_inputs(seed + 1).items():
        if name != "x":
            out[name + "_2"] = value
    return out


def reference(
    x, c, w_ada, b_ada, norm1_g, w_in, mu_shift, w0, w2, a0, a2, g2, k_k, k_a, r_k, ln_x_w,
    ln_x_b, pool_w, pool_b, pool_scale, w_out, norm2_g, w_up, conv_w, conv_b, w_down, norm_f_g,
    norm_mix_g_2, w_in_2, b_gate_2, conv_a_w_2, w_out_a_2, sink_logits_2, w_o_attn_2,
    w_mix_out_2, norm_ffn_g_2, ffn_w_up_2, ffn_conv_w_2, ffn_conv_b_2, ffn_w_down_2,
    norm_final_g_2,
):
    x = first_block(
        x, c, w_ada, b_ada, norm1_g, w_in, mu_shift, w0, w2, a0, a2, g2, k_k, k_a, r_k, ln_x_w,
        ln_x_b, pool_w, pool_b, pool_scale, w_out, norm2_g, w_up, conv_w, conv_b, w_down,
        norm_f_g,
    )
    return second_block(
        x, norm_mix_g_2, w_in_2, b_gate_2, conv_a_w_2, w_out_a_2, sink_logits_2, w_o_attn_2,
        w_mix_out_2, norm_ffn_g_2, ffn_w_up_2, ffn_conv_w_2, ffn_conv_b_2, ffn_w_down_2,
        norm_final_g_2,
    )


_drawn_inputs = setup_inputs


def setup_inputs(seed=0):
    import zlib

    import numpy as np

    out = dict(_drawn_inputs(seed))
    spreads = {}
    factors = {'a0': 3.887,
     'ln_x_w': 3.633,
     'ln_x_b': 8.0,
     'pool_b': 8.0,
     'conv_b': 7.147,
     'norm_mix_g_2': 2.962,
     'b_gate_2': 8.0,
     'sink_logits_2': 64.0,
     'norm_ffn_g_2': 14.03,
     'ffn_conv_b_2': 13.757,
     'norm_final_g_2': 7.875}
    for name, (base, spread) in spreads.items():
        noise = np.random.default_rng([zlib.crc32(name.encode()), seed]).standard_normal(out[name].shape)
        drawn = base * np.exp(spread * noise) if base else spread * noise
        out[name] = jnp.asarray(drawn.astype(out[name].dtype))
    for name, factor in factors.items():
        out[name] = (out[name] * factor).astype(out[name].dtype)
    return out
```

```python
from contextlib import ExitStack

import concourse.bass as bass
from concourse import mybir

ALU = mybir.AluOpType
ACT = mybir.ActivationFunctionType
AX = mybir.AxisListType
F32 = mybir.dt.float32
F32R = mybir.dt.float32r

P = 128
T = 256
DM = 2048
KT = DM // P
HEAD = 64
DR = DM // 2
NR = DR // P
DFF = 5632
NF = DFF // P
NPOOL = 4
GATE = 160
LORA = 64
CH = 64
CHUNK = 2048
HALF = CHUNK // 2
RING = 4
DKT = 15
NGROUP = 4
NQ = 16
NKV = 4
RMS_EPS = 1e-6
GN_EPS = 64e-5
L2_EPS = 1e-12
EXP_HALF = 0.6065306597126334
MASKED = -1.0e30

ADA0 = 2 * KT
LORA_CHUNKS = 3
WKV_CHUNKS = 8
WKV_RAW = 24
PHASES = [("lora", 3), ("wkv", 32), ("wout", 16), ("up1", 88), ("down1", 48), ("qkv", 12), ("cvb", 24),
          ("gates", 32), ("ao", 16), ("mix", 16), ("up2", 88), ("down2", 48)]
FIRST_CHUNK = {}
_n = 0
for _name, _count in PHASES:
    FIRST_CHUNK[_name] = _n
    _n += _count
N_WEIGHT_CHUNKS = _n
WKV0 = ADA0 + LORA_CHUNKS
WKV_LOOP = WKV0 + 1
RAW = []
for _c in range(N_WEIGHT_CHUNKS):
    _w = _c - FIRST_CHUNK["wkv"]
    RAW.append(ADA0 + _c if _w <= 0 else WKV0 - 2 + 3 * _w if _w <= WKV_CHUNKS * NGROUP else RAW[-1] + (3 if _w == WKV_CHUNKS * NGROUP + 1 else 1))
N_RAW = RAW[-1] + 1


def ada_raw(n):
    return WKV0 + 3 * (n // 2) + 2 + n % 2


TILES = {"lora": 3, "wkv": 32, "wout": 16, "up1": 88, "down1": 16, "qkv": 12, "cvb": 24, "gates": 32, "ao": 32,
         "mix": 16, "up2": 88, "down2": 16}
FIRST_TILE = {}
_n = 0
for _name, _ in PHASES:
    FIRST_TILE[_name] = _n
    _n += TILES[_name]

PARAMS = [("c", KT), ("b_ada", 6 * KT), ("norm1_g", KT), ("mu", 27), ("w0", NR), ("a0", NR), ("k_k", NR), ("k_a", NR),
          ("r_k", NR), ("ln_w", NR), ("ln_b", NR), ("pool_b", NR), ("pool_scale", NR), ("norm2_g", KT),
          ("conv_w", 3 * 2 * NF), ("conv_b", 2 * NF), ("norm_f_g", KT), ("norm_mix_g", KT), ("b_gate", 2 * KT),
          ("conv_a_w", 3 * NR), ("norm_ffn_g", KT), ("conv2_w", 3 * 2 * NF), ("conv2_b", 2 * NF),
          ("norm_final_g", KT), ("sink", NQ)]
PCOL = {}
_n = 0
for _name, _count in PARAMS:
    PCOL[_name] = _n
    _n += _count
N_PARAM = _n
C_RES = {"ident": 0, "ones": 128, "headones": 256, "eps": 384, "rms_eps": 384, "gn_eps": 385}
N_CRES = 386
C_WKV = {"prod": 0, "level": 256, "eye": 640, "scan": 704}
N_CWKV = 960
C_ATT = {"cos": 0, "sin": 256, "rot": 512, "band": 640}
N_CATT = 1152
SCRATCH = 2048
LORA_AT = {0: (0, 1), 2: (2,), 4: (3,)}
WKV_LINKS = 22


def blocks_program(nc, stream, x_in, param_in, lora_in, pool_w_in, pool_inv_in, res_in, wkv_in, att_in, out):
    with ExitStack() as ctx:
        def sb(name, shape, dt=F32):
            return ctx.enter_context(nc.sbuf_tensor(name, shape, dt))

        def sem(name):
            return ctx.enter_context(nc.semaphore(name))

        raw = sb("raw", [P, RING, KT, P])
        whi = sb("whi", [P, RING, KT // 2, P], F32R)
        wlo = sb("wlo", [P, RING, KT // 2, P], F32R)
        ahi = sb("ahi", [P, KT, T], F32R)
        alo = sb("alo", [P, KT, T], F32R)
        x = sb("x", [P, KT, T])
        par = sb("par", [P, N_PARAM])
        res = sb("res", [P, N_CRES])
        mod = sb("mod", [P, 6, KT])
        gs = sb("gs", [P, 2, KT])
        om_mu = sb("om_mu", [P, 27])
        om_ka = sb("om_ka", [P, NR])
        pbs = sb("pbs", [P, NR])
        crep = sb("crep", [P, KT, 32])
        ada_row = sb("ada_row", [P, 512])
        ssq = sb("ssq", [P, T])
        rstd = sb("rstd", [P, T])
        wssq = sb("wssq", [P, T])
        yb = sb("yb", [P, 4, T])
        ft = sb("ft", [P, 2, T])
        small = sb("small", [P, 32])

        base = -(-nc.sbuf_base // 32) * 32
        end = nc.sbuf_usable_end

        def layout(at=0):
            top = [at]

            def place(name, shape, dt=F32):
                n = 4
                for d in shape[1:]:
                    n *= d
                assert base + top[0] + n <= end, (name, base + top[0] + n - end)
                t = nc.alloc_sbuf_tensor_at(name, shape, dt, offset=base + top[0])
                where, top[0] = top[0], top[0] + -(-n // 32) * 32
                places[name] = where
                return t

            return place

        places = {}
        ffn = layout()
        ffhi = ffn("ffhi", [P, NF, T], F32R)
        fflo = ffn("fflo", [P, NF, T], F32R)
        rec = layout()
        mix = rec("mix", [P, KT, T])
        g_sb = rec("g_sb", [P, NR, T])
        aa = rec("aa", [P, NR, T])
        kraw = rec("kraw", [P, 2, T])
        rraw = rec("rraw", [P, 2, T])
        vraw = rec("vraw", [P, 2, T])
        ar = rec("ar", [P, 2, 4, 2, CH])
        bk = rec("bk", [P, 2, 2, T])
        nb = rec("nb", [P, 8, 4, CH])
        tinv = rec("tinv", [P, 8, CH])
        tinvt = rec("tinvt", [P, 8, CH])
        zmat = rec("zmat", [P, 8, CH])
        tok = rec("tok", [P, 4, 3, P])
        bm = rec("bm", [P, 2, 8, CH])
        rs = rec("rs", [P, 4, CH])
        us = rec("us", [P, 4, CH])
        av = rec("av", [P, 2, 4, CH])
        state = rec("state", [P, 2, 2, P])
        ep = rec("ep", [P, 2, T])
        ea = rec("ea", [P, 2, T])
        en = rec("en", [P, 2, T])
        t2 = rec("t2", [P, 2, T])
        dc = rec("dc", [P, 2, 4])
        cw = rec("cw", [P, N_CWKV])
        kk, bv, t1 = yb[:, 0:2], yb[:, 2:4], ft[:, :]
        lora_w = layout(places["nb"])("lora_w", [P, 3, DR])
        lora_x = layout(places["tok"])("lora_x", [P, 3, T])
        pool_w = layout(places["aa"])("pool_w", [P, NPOOL, 2, 2, P])
        pool_inv = layout(places["kraw"])("pool_inv", [P, NPOOL, T])
        pads = layout(places["ep"])
        pad_a = pads("pad_a", [P, 2, 16 + T])
        pad_b = pads("pad_b", [P, 2, 16 + T])
        att = layout()
        qkv = att("qkv", [P, 12, T])
        gates = att("gates", [P, 2 * KT, T])
        yahi = att("yahi", [P, NR, T], F32R)
        yalo = att("yalo", [P, NR, T], F32R)
        oahi = att("oahi", [P, NR, T], F32R)
        oalo = att("oalo", [P, NR, T], F32R)
        qr = att("qr", [P, T])
        vtok = att("vtok", [P, 2, 2 * P])
        prob = att("prob", [P, 2, 2, T])
        catt = att("catt", [P, N_CATT])
        pt = yb

        ident = res[:, 0:128]
        ones = res[:, 128:256]
        headones = res[:, 256:384]
        rms_eps = res[:, 384:385]
        gn_eps = res[:, 385:386]
        prodmask = cw[:, 0:256]
        eye = cw[:, 640:704]
        scanmask = cw[:, 704:960]
        cos, sin = catt[:, 0:256], catt[:, 256:512]
        rot, band = catt[:, 512:640], catt[:, 640:1152]

        bank = [ctx.enter_context(nc.psum_tensor(f"bank{n}", [P, 512], F32)) for n in range(8)]
        aux, ada = bank[2], bank[3]
        work = bank[4:8]

        raw_full = [sem(f"raw_full{n}") for n in range(RING)]
        x_loaded, par_loaded, res_loaded = sem("x_loaded"), sem("par_loaded"), sem("res_loaded")
        lora_loaded, wkv_loaded = sem("lora_loaded"), sem("wkv_loaded")
        pool_loaded, att_loaded = sem("pool_loaded"), sem("att_loaded")
        out_stored = sem("out_stored")
        hi_ready, lo_ready, half_used, tile_free = sem("hi_ready"), sem("lo_ready"), sem("half_used"), sem("tile_free")
        ada_used, ada_copied, ada_turned, mod_ready = sem("ada_used"), sem("ada_copied"), sem("ada_turned"), sem("mod_ready")
        crep_ready, derived = sem("crep_ready"), sem("derived")
        sq_ready, ssq_ready, stat_ready, std_ready = sem("sq_ready"), sem("ssq_ready"), sem("stat_ready"), sem("std_ready")
        normed, ahi_ready, a_ready = sem("normed"), sem("ahi_ready"), sem("a_ready")
        xnew = sem("xnew")
        scaled, gated, silu_ready = sem("scaled"), sem("gated"), sem("silu_ready")
        ffhi_ready, ff_ready = sem("ffhi_ready"), sem("ff_ready")
        dve_chain, pool_chain = sem("dve_chain"), sem("pool_chain")
        second_mean, second_std = sem("second_mean"), sem("second_std")
        pe_held, pool_held = sem("pe_held"), sem("pool_held")
        lora_act, lora_mm, lora_out = sem("lora_act"), sem("lora_mm"), sem("lora_out")
        cumulated, decays, kk_sq, kk_sum, kk_norm = sem("cumulated"), sem("decays"), sem("kk_sq"), sem("kk_sum"), sem("kk_norm")
        bonus_in, bonus_sum, prep_done = sem("bonus_in"), sem("bonus_sum"), sem("prep_done")
        products, products_masked, turned, tok_ready = sem("products"), sem("products_masked"), sem("turned"), sem("tok_ready")
        level_ready, level_z, level_zs, level_t, level_done = (
            sem("level_ready"), sem("level_z"), sem("level_zs"), sem("level_t"), sem("level_done"))
        state_zero, r_mm, r_ready, u_mm, u_ready = sem("state_zero"), sem("r_mm"), sem("r_ready"), sem("u_mm"), sem("u_ready")
        s_mm, s_ready, y_mm, y_ready = sem("s_mm"), sem("s_ready"), sem("y_mm"), sem("y_ready")
        mean_sum, centred, var_in, var_sum, gn_std, gn_out, mixed = (
            sem("mean_sum"), sem("centred"), sem("var_in"), sem("var_sum"), sem("gn_std"), sem("gn_out"), sem("mixed"))
        pool_z, pool_mm, pool_out = sem("pool_z"), sem("pool_mm"), sem("pool_out")
        rot_mm, roped, vt_mm, vt_ready = sem("rot_mm"), sem("roped"), sem("vt_mm"), sem("vt_ready")
        score_mm, masked, shifted, expd, divided = sem("score_mm"), sem("masked"), sem("shifted"), sem("expd"), sem("divided")
        av_mm, av_ready = sem("av_mm"), sem("av_ready")
        kk_half, kk_raw, normed_y, convolved = sem("kk_half"), sem("kk_raw"), sem("normed_y"), sem("convolved")
        yahi_ready, ya_ready, merged = sem("yahi_ready"), sem("ya_ready"), sem("merged")
        pt_mm, pt_ready, o_mm, oahi_ready, oa_ready = sem("pt_mm"), sem("pt_ready"), sem("o_mm"), sem("oahi_ready"), sem("oa_ready")

        def tile_bank(t):
            for phase in ("up1", "up2"):
                n = t - FIRST_TILE[phase]
                if 0 <= n < TILES[phase]:
                    return bank[(0, 1, 4, 5)[n % 4]][:, 0:T]
            return bank[t % 2][:, 0:T]

        def pcol(name, n, count=1):
            return par[:, bass.ds(PCOL[name] + n, count)] if not isinstance(n, int) else par[:, PCOL[name] + n:PCOL[name] + n + count]

        def one(t, n):
            if isinstance(n, int):
                return t[:, n]
            return t[:, bass.ds(n, 1)].rearrange("p o n -> p (o n)")

        def col(t, n):
            return t[:, n:n + 1] if isinstance(n, int) else t[:, bass.ds(n, 1)]

        def flat(t):
            return t.rearrange("p a b -> p (a b)")

        def kept(t, n):
            return t[:, n:n + 2] if isinstance(n, int) else t[:, bass.ds(n, 2)]

        FILLS = ["h1", "mixed", "h2", "u1", "gmix", "u2"]
        SUMS = ["x0", "x1", "x2", "x4", "x5"]
        READ_BEFORE = {"h1": 0, "mixed": 2 * (FIRST_CHUNK["wout"]), "h2": 2 * FIRST_CHUNK["up1"],
                       "u1": 2 * FIRST_CHUNK["qkv"], "gmix": 2 * FIRST_CHUNK["ao"], "u2": 2 * FIRST_CHUNK["up2"]}

        def make_chain(eng, counter):
            now = {"n": 0, "i": 0, "per": 0, "due": 0}

            def link(ins):
                now["n"] += 1
                ins.then_inc(counter, 1)
                eng.wait_ge(counter, now["n"] + now["per"] * now["i"])

            def enter(i, start, per):
                now["due"] = now["n"] + per
                now["n"] -= per * start
                now["i"], now["per"] = i, per

            def leave(start, times):
                per = now["per"]
                now["n"] += per * start
                assert now["n"] == now["due"], f"{now['n'] - now['due']} links more in the loop's body than said"
                now["n"] += per * (times - 1)
                now["i"], now["per"] = 0, 0

            return link, enter, leave

        block = ctx.enter_context(nc.Block())

        @block.sync
        def _(sp):
            sp.dma_start(par[:], param_in).then_inc(par_loaded, 16)
            sp.dma_start(res[:], res_in).then_inc(res_loaded, 16)

            def load(r):
                static, i, per = r
                dst = raw[:, static % RING].rearrange("p k n -> p (k n)")
                if isinstance(i, int):
                    src = stream[static + per * i]
                else:
                    src = stream[bass.ds(per * i + static, 1)].rearrange("o p n -> p (o n)")
                sp.dma_start(dst, src).then_inc(raw_full[static % RING], 16)

            for r in range(2):
                load((r, 0, 0))
            sp.dma_start(x[:], x_in).then_inc(x_loaded, 16)
            for r in range(2, RING):
                load((r, 0, 0))

            with sp.Fori(1, ADA0 // RING) as i:
                for q in range(RING):
                    sp.wait_ge(ada_used, RING * i + (q - 3))
                    load((q, i, RING))
            for r in range(ADA0, ADA0 + RING):
                sp.wait_ge(ada_used, r - RING + 1)
                load((r, 0, 0))
            sp.dma_start(lora_w[:], lora_in).then_inc(lora_loaded, 16)
            sp.dma_start(cw[:], wkv_in).then_inc(wkv_loaded, 16)
            kind = {RAW[c]: ("w", c) for c in range(N_WEIGHT_CHUNKS)}
            kind |= {r: ("ada", n) for n, r in enumerate(r for r in range(N_RAW) if r not in kind)}

            def wkv_loads(i):
                for q in range(WKV_RAW):
                    was, n = kind[WKV_LOOP + (0 if isinstance(i, int) else WKV_RAW) + q - RING]
                    lead = 0 if isinstance(i, int) else 1
                    if was == "w":
                        sp.wait_ge(lo_ready, 2 * (n - lead * WKV_CHUNKS) + 2 + 2 * WKV_CHUNKS * i)
                    else:
                        sp.wait_ge(ada_used, n - lead * KT + 1 + KT * i)
                    load((WKV_LOOP + q, i, WKV_RAW))

            assert WKV_LOOP == ADA0 + RING
            wkv_loads(0)
            with sp.Fori(1, NGROUP) as i:
                wkv_loads(i)
            first = WKV_LOOP + NGROUP * WKV_RAW
            c0 = FIRST_CHUNK["wout"] + 1
            assert RAW[c0] == first
            for r in range(first, first + RING):
                was, n = kind[r - RING]
                if was == "w":
                    sp.wait_ge(lo_ready, 2 * n + 2)
                else:
                    sp.wait_ge(ada_used, n + 1)
                load((r, 0, 0))
            count = (N_RAW - first) // RING
            with sp.Fori(1, count) as i:
                for q in range(RING):
                    sp.wait_ge(lo_ready, 2 * (c0 + q) - 6 + 2 * RING * i)
                    load((first + q, i, RING))
            for q in range((N_RAW - first) % RING):
                sp.wait_ge(lo_ready, 2 * (c0 + q) - 6 + 2 * RING * count)
                load((first + q + RING * count, 0, 0))
            sp.wait_ge(out_stored, 16)

        @block.tensor
        def _(pe):
            def product(k, i, dh, t, blocks, hi, lo, starts, stops, ready=None):
                pe.wait_ge(lo_ready, k + 1 + dh * i)
                for n, (b, kt) in enumerate(blocks):
                    if ready is not None:
                        pe.wait_ge(a_ready, ready + kt + 1)
                    wh, wl = whi[:, k % RING, b], wlo[:, k % RING, b]
                    last = n == len(blocks) - 1
                    nc.tensor.matmul(tile_bank(t), wh, hi[:, kt], start=starts and n == 0, stop=False)
                    nc.tensor.matmul(tile_bank(t), wh, lo[:, kt], start=False, stop=False)
                    mm = nc.tensor.matmul(tile_bank(t), wl, hi[:, kt], start=False, stop=stops and last)
                mm.then_inc(half_used, 1)

            def tile_wait(t, i, dt, banks=2):
                if t >= 2:
                    pe.wait_ge(tile_free, t + 1 - banks + dt * i)

            def full_half(phase, n, i, per_iter, fill=None):
                k = 2 * FIRST_CHUNK[phase] + n
                t = FIRST_TILE[phase] + n // 2
                if n % 2 == 0:
                    tile_wait(t, i, per_iter, 4 if phase in ("up1", "up2") else 2)
                ready = 16 * FILLS.index(fill) if fill is not None and n < 2 else None
                product(k, i, 2 * per_iter, t, [(b, 8 * (n % 2) + b) for b in range(8)], ahi, alo,
                        n % 2 == 0, n % 2 == 1, ready)

            def ada_chunk(static, i, per, kt):
                r, n = static
                pe.wait_ge(raw_full[r % RING], 16 * (r // RING + 1) + 16 * (per // RING) * i)
                if kt == 0:
                    if isinstance(i, int):
                        if n // KT + i:
                            pe.wait_ge(ada_copied, n // KT + i)
                    else:
                        pe.wait_ge(ada_copied, n // KT + i)
                src = raw[:, r % RING].rearrange("p k n -> p (k n)")
                for g in range(4):
                    mm = nc.tensor.matmul(ada[32 * g:32 * g + 32, :], crep[:, kt], src[:, 512 * g:512 * g + 512],
                                          start=kt == 0, stop=kt == KT - 1, tile_position=(0, 32 * g))
                mm.then_inc(ada_used, 1)

            def ada_turn(n, i):
                pe.wait_ge(ada_copied, n + 1 + i)
                for b in range(4):
                    mm = nc.tensor.transpose(aux[:, b * P:(b + 1) * P], ada_row[:, b * P:(b + 1) * P], ident)
                mm.then_inc(ada_turned, 1)

            def stat(name):
                pe.wait_ge(ssq_ready, 17 * (SUMS.index(name) + 1))
                mm = nc.tensor.matmul(aux[:, 0:T], ones, ssq[:], start=True, stop=True)
                if name == "x2":
                    mm = nc.tensor.matmul(aux[:, T:2 * T], ones, wssq[:], start=True, stop=True)
                mm.then_inc(stat_ready, 1)

            pe.wait_ge(res_loaded, 16)
            pe.wait_ge(crep_ready, 1)
            for v in range(2):
                for kt in range(KT):
                    ada_chunk((KT * v + kt, KT * v + kt), 0, 0, kt)
                if v == 0:
                    ada_turn(0, 0)
                else:
                    pe.wait_ge(mod_ready, 1)
                    ada_turn(1, 0)
            pe.wait_ge(mod_ready, 2)
            stat("x0")

            for n in range(2 * LORA_CHUNKS):
                full_half("lora", n, 0, 0, "h1")

            def lora_decay(j):
                if j >= 2:
                    pe.wait_ge(lora_out, 4 * (j - 2) + 4)
                for w, rows in enumerate((slice(0, LORA), slice(LORA, P))):
                    for p in range(2):
                        d = (2 * j + p) * P
                        mm = nc.tensor.matmul(work[2 * (j % 2) + w][:, p * T:(p + 1) * T], lora_w[rows, 0, d:d + P],
                                              lora_x[rows, 0], start=True, stop=True)
                mm.then_inc(lora_mm, 1)

            def lora_gate(j):
                pe.wait_ge(lora_out, 12 if j < 2 else 16)
                for p in range(2):
                    d = (2 * j + p) * P
                    dst = work[j % 4][:, p * T:(p + 1) * T]
                    nc.tensor.matmul(dst, lora_w[:, 1, d:d + P], lora_x[:, 1], start=True, stop=False)
                    mm = nc.tensor.matmul(dst, lora_w[0:GATE - P, 2, d:d + P], lora_x[0:GATE - P, 2],
                                          start=False, stop=True)
                mm.then_inc(lora_mm, 1)

            def hold(signal, value):
                pe.wait_ge(signal, value)
                pe.sem_inc(pe_held, 1)

            def products_step(g):
                hold(prep_done, g + 1)
                for m in range(8):
                    q, p, hh = m // 4, m // 2 % 2, m % 2
                    rows = slice(64 * q, 64 * q + 64)
                    for e in range(2):
                        c = 2 * hh + e
                        for w in range(2):
                            dst = work[m // 2][64 * e:64 * e + 64, (m % 2) * 256 + w * 128:(m % 2) * 256 + w * 128 + 128]
                            mm = nc.tensor.matmul(dst, bk[rows, p, w, c * CH:(c + 1) * CH],
                                                  ar[rows, p, c].rearrange("p a t -> p (a t)"), start=True, stop=True,
                                                  tile_position=(64 * q, 64 * e))
                    if m % 2 == 1:
                        mm.then_inc(products, 1)

            def turn_step(g):
                pe.wait_ge(products_masked, 4 * g + 4)
                for n in range(12):
                    ph, w = n // 3, n % 3
                    p, hh = ph // 2, ph % 2
                    cols = slice(hh * P, hh * P + P)
                    src = vraw[:, p, cols] if w == 2 else bk[:, p, w, cols]
                    mm = nc.tensor.transpose(work[n // 4][:, (n % 4) * P:(n % 4 + 1) * P], src, ident)
                    if n % 4 == 3:
                        mm.then_inc(turned, 1)

            def pairs():
                for m in range(8):
                    for e in range(2):
                        yield m, slice(64 * e, 64 * e + 64), (64 * e, 64 * e)

            def z_step(g, level):
                hold(level_ready, 6 * g + level + 1)
                if level == 0:
                    for m, e, at in pairs():
                        mm = nc.tensor.matmul(work[3][e, m * CH:(m + 1) * CH], bm[e, 0, m], eye[e, :], start=True,
                                              stop=True, tile_position=at)
                else:
                    hold(level_done, 6 * g + level)
                    if level == 1:
                        hold(tok_ready, 3 * g + 3)
                    for m, e, at in pairs():
                        mm = nc.tensor.matmul(work[0][e, m * CH:(m + 1) * CH], bm[e, level % 2, m], tinvt[e, m], start=True,
                                              stop=True, tile_position=at)
                mm.then_inc(level_z, 1)

            def t_step(g, level):
                hold(level_zs, 5 * g + level)
                if level < 5:
                    for m, e, at in pairs():
                        mm = nc.tensor.matmul(work[2][e, m * CH:(m + 1) * CH], tinv[e, m], zmat[e, m], start=True,
                                              stop=True, tile_position=at)
                    mm.then_inc(level_t, 1)
                for m, e, at in pairs():
                    mm = nc.tensor.matmul(work[1][e, m * CH:(m + 1) * CH], zmat[e, m], tinv[e, m], start=True, stop=True,
                                          tile_position=at)
                mm.then_inc(level_t, 1)

            def rows_of(c):
                hh, e = c // 2, c % 2
                return 64 * e, [(4 * q + 2 * p + hh, p, q, 2 * p + hh) for p in range(2) for q in range(2)]

            def av_step(g):
                hold(level_done, 6 * g + 1)
                for c in range(4):
                    e, heads = rows_of(c)
                    for m, p, q, ph in heads:
                        at = ((c // 2) * 4 + 2 * p + q) * CH
                        mm = nc.tensor.matmul(work[3][e:e + 64, at:at + CH], nb[e:e + 64, m, 2],
                                              tok[e:e + 64, ph, 2, 64 * q:64 * q + 64], start=True, stop=True,
                                              tile_position=(e, e))
                mm.then_inc(av_mm, 1)

            def r_step(g, c):
                if c == 0:
                    hold(state_zero, g + 1)
                    hold(level_done, 6 * g + 6)
                else:
                    hold(s_ready, 3 * g + c)
                e, _ = rows_of(c)
                for p in range(2):
                    mm = nc.tensor.matmul(work[0][e:e + 64, p * P:(p + 1) * P], ar[:, p, c, 0], state[:, c % 2, p],
                                          start=True, stop=True, tile_position=(0, e))
                mm.then_inc(r_mm, 1)

            def u_step(g, c):
                hold(r_ready, 4 * g + c + 1)
                e, heads = rows_of(c)
                for m, p, q, ph in heads:
                    at = (2 * p + q) * CH
                    mm = nc.tensor.matmul(work[1][e:e + 64, at:at + CH], tinv[e:e + 64, m], rs[e:e + 64, 2 * p + q],
                                          start=True, stop=True, tile_position=(e, e))
                mm.then_inc(u_mm, 1)

            def s_step(g, c):
                hold(u_ready, 4 * g + c + 1)
                e, _ = rows_of(c)
                for p in range(2):
                    dst = work[2][:, p * P:(p + 1) * P]
                    ph = 2 * p + c // 2
                    nc.tensor.matmul(dst, tok[e:e + 64, ph, 1], tok[e:e + 64, ph, 2], start=True, stop=False,
                                     tile_position=(e, 0))
                    nc.tensor.matmul(dst, tok[e:e + 64, ph, 0], us[e:e + 64, 2 * p:2 * p + 2].rearrange("p h t -> p (h t)"),
                                     start=False, stop=False, tile_position=(e, 0))
                    mm = nc.tensor.matmul(dst, ident, state[:, c % 2, p], start=False, stop=True, tile_position=(0, 0))
                mm.then_inc(s_mm, 1)

            def y_step(g, c):
                hold(u_ready, 4 * g + c + 1)
                if c == 0:
                    hold(av_ready, g + 1)
                e, heads = rows_of(c)
                for m, p, q, ph in heads:
                    cols = slice(p * T + c * CH, p * T + (c + 1) * CH)
                    if q == 0:
                        nc.tensor.matmul(work[3][:, cols], state[:, c % 2, p], ar[:, p, c, 1], start=True, stop=False,
                                         tile_position=(0, 0))
                    dst = work[3][64 * q:64 * q + 64, cols]
                    nc.tensor.matmul(dst, tok[e:e + 64, ph, 2, 64 * q:64 * q + 64], nb[e:e + 64, m, 3], start=False,
                                     stop=False, tile_position=(e, 64 * q))
                    mm = nc.tensor.matmul(dst, us[e:e + 64, 2 * p + q], nb[e:e + 64, m, 1], start=False, stop=True,
                                          tile_position=(e, 64 * q))
                mm.then_inc(y_mm, 1)

            def head_sum(src):
                return nc.tensor.matmul(aux[:, :], headones, flat(src[:, :]), start=True, stop=True)

            def mean_step(g):
                pe.wait_ge(y_ready, g + 1)
                if isinstance(g, int):
                    pe.wait_ge(mod_ready, 6)
                else:
                    pe.wait_ge(kk_norm, g + 2)
                head_sum(t2).then_inc(mean_sum, 1)

            def var_step(g):
                pe.wait_ge(var_in, g + 1)
                head_sum(zmat).then_inc(var_sum, 1)

            def kk_step(g):
                pe.wait_ge(kk_sq, g + 1)
                pe.wait_ge(mod_ready, g + 2)
                head_sum(t2).then_inc(kk_sum, 1)

            def bonus_step(g, first):
                pe.wait_ge(bonus_in, g + 1)
                if not first:
                    pe.wait_ge(gn_std, g)
                head_sum(t1).then_inc(bonus_sum, 1)

            def recurrence_step(n, g):
                first = {0: (products_step, ()), 1: (z_step, (0,)), 2: (t_step, (1,)), 3: (t_step, (2,)),
                         4: (t_step, (3,)), 5: (t_step, (4,)), 6: (t_step, (5,)), 7: (u_step, (0,)),
                         8: (r_step, (1,)), 10: (u_step, (2,)), 11: (r_step, (3,)), 13: (var_step, ())}
                between = {3: av_step}
                then = {0: (turn_step, ()), 1: (z_step, (1,)), 2: (z_step, (2,)), 3: (z_step, (3,)), 4: (z_step, (4,)),
                        5: (z_step, (5,)), 6: (r_step, (0,)), 8: (u_step, (1,)), 9: (r_step, (2,)), 11: (u_step, (3,)),
                        12: (mean_step, ())}
                states = {(7, 1): 0, (9, 0): 1, (10, 1): 2}
                for part, steps in ((0, first), (1, then)):
                    if n in steps:
                        step, more = steps[n]
                        step(g, *more)
                    if part == 0 and n in between:
                        between[n](g)
                    if (n, part) in states:
                        s_step(g, states[n, part])
                        y_step(g, states[n, part])
                    if (n, part) == (12, 0):
                        y_step(g, 3)
                    yield part

            def wkv_body(i, g, opening):
                for n in range(16):
                    steps = recurrence_step(n, g) if not opening else iter((0, 1))
                    full_half("wkv", n, i, WKV_CHUNKS)
                    if opening:
                        for j in LORA_AT.get(n, ()):
                            if j == 0:
                                pe.wait_ge(lora_loaded, 16)
                                pe.wait_ge(lora_act, 3)
                            lora_decay(j)
                        if 5 <= n <= 8:
                            lora_gate(n - 5)
                    next(steps)
                    ada_chunk((ada_raw(n), 2 * KT + n), i, WKV_RAW, n)
                    next(steps)
                    if n == 6:
                        kk_step(i)
                    if n == 14:
                        bonus_step(i, opening)
                pe.wait_ge(prep_done, i + 1)
                ada_turn(2, i)

            wkv_body(0, 0, True)
            with pe.Fori(1, NGROUP) as i:
                wkv_body(i, i - 1, False)
            g = NGROUP - 1
            for n in range(16):
                for _ in recurrence_step(n, g):
                    pass
            pe.wait_ge(pool_loaded, 32)
            for j in range(NPOOL):
                pe.wait_ge(pool_z, j + 1)
                if j == 0:
                    pe.wait_ge(y_ready, NGROUP)
                for d in range(2):
                    for k in range(2):
                        mm = nc.tensor.matmul(work[j][:, d * T:(d + 1) * T], pool_w[:, j, k, d], mix[:, NR + 2 * j + k],
                                              start=k == 0, stop=k == 1)
                mm.then_inc(pool_mm, 1)

            def loop(phase, body, times, fill):
                with pe.Fori(0, times) as i:
                    for n in range(2 * body):
                        full_half(phase, n, i, body, fill)

            def down(phase):
                def body(i):
                    for j in range(4):
                        t = FIRST_TILE[phase] + j
                        tile_wait(t, i, 4)
                        for c in range(3):
                            k0 = 2 * (FIRST_CHUNK[phase] + 3 * j + c)
                            n = min(NF - DKT * c, DKT)
                            product(k0, i, 24, t, [(b, DKT * c + b) for b in range(8)], ffhi, fflo, c == 0, False)
                            product(k0 + 1, i, 24, t, [(b - 8, DKT * c + b) for b in range(8, n)], ffhi, fflo,
                                    False, c == 2)
                with pe.Fori(0, 4) as i:
                    body(i)

            loop("wout", 4, 4, "mixed")
            stat("x1")
            loop("up1", 4, 22, "h2")
            pe.wait_ge(ff_ready, NF)
            down("down1")
            stat("x2")
            for n in range(24):
                full_half("qkv", n, 0, 0, "u1")
            loop("cvb", 12, 2, None)

            pe.wait_ge(att_loaded, 16)
            pe.wait_ge(tile_free, FIRST_TILE["cvb"])
            for p in range(2):
                mm = nc.tensor.matmul(work[0][:, p * T:(p + 1) * T], rot, qkv[:, 8 + p], start=True, stop=True)
            mm.then_inc(rot_mm, 1)
            for s in range(2):
                for p in range(2):
                    mm = nc.tensor.transpose(work[1][:, s * 256 + p * P:s * 256 + (p + 1) * P],
                                             qkv[:, 10 + p, s * P:(s + 1) * P], ident)
            mm.then_inc(vt_mm, 1)

            def attend(n, i, kv):
                j = 4 * kv + i
                if n == 0:
                    pe.wait_ge(roped, j + 2)
                    nc.tensor.matmul(work[0][:, 0:T], rot, one(qkv, 4 * kv + i), start=True, stop=True).then_inc(rot_mm, 1)
                if n == 1:
                    pe.wait_ge(roped, j + 3)
                    if not isinstance(j, int) or j:
                        pe.wait_ge(pt_ready, 2 * j)
                    pe.wait_ge(vt_ready, 1)
                    for e in range(2):
                        for b in range(2):
                            mm = nc.tensor.matmul(work[1 + e][:, b * T:(b + 1) * T], qr[64 * e:64 * e + 64, b * P:(b + 1) * P],
                                                  qkv[64 * e:64 * e + 64, 8 + kv], start=True, stop=True)
                        mm.then_inc(score_mm, 1)
                if n == 4:
                    pe.wait_ge(divided, j + 1)
                    for e in range(2):
                        for b in range(2):
                            for s in range(2):
                                mm = nc.tensor.transpose(work[1 + e][:, s * T + b * P:s * T + (b + 1) * P],
                                                         prob[:, e, b, s * P:(s + 1) * P], ident)
                        mm.then_inc(pt_mm, 1)
                if n == 6:
                    pe.wait_ge(pt_ready, 2 * j + 2)
                    if not isinstance(j, int) or j:
                        pe.wait_ge(oa_ready, j)
                    for e in range(2):
                        for s in range(2):
                            c = 128 * kv + 64 * e
                            mm = nc.tensor.matmul(work[3][64 * e:64 * e + 64, 0:T], vtok[:, s, c:c + 64],
                                                  pt[:, 2 * e + s], start=s == 0, stop=s == 1)
                    mm.then_inc(o_mm, 1)

            for kv in range(2):
                def body(i, kv=kv):
                    for n in range(8):
                        full_half("gates", 32 * kv + n, i, 4)
                        attend(n, i, kv)
                if kv == 0:
                    body(0)
                with pe.Fori(1 - kv, 4) as i:
                    body(i)

            pe.wait_ge(oa_ready, NR)
            pe.wait_ge(ya_ready, NR)
            with pe.Fori(0, 4) as i:
                for n in range(8):
                    k = 2 * FIRST_CHUNK["ao"] + n
                    t = FIRST_TILE["ao"] + n
                    tile_wait(t, i, 8)
                    hi, lo = (yahi, yalo) if n % 2 == 0 else (oahi, oalo)
                    product(k, i, 8, t, [(b, b) for b in range(8)], hi, lo, True, True)
            loop("mix", 4, 4, "gmix")
            stat("x4")
            loop("up2", 4, 22, "u2")
            pe.wait_ge(ff_ready, 2 * NF)
            down("down2")
            stat("x5")

        SCALED = {"lora": 0, "wkv": 3, "up1": 3 + 6 * NGROUP, "up2": 3 + 6 * NGROUP + 2 * NF}

        @block.scalar
        def _(act):
            def cut_hi(k, i=0, dh=0, dr=0):
                if isinstance(i, int) and k + dh * i >= 2 * N_WEIGHT_CHUNKS:
                    return
                r = RAW[k // 2] if k // 2 < N_WEIGHT_CHUNKS else N_RAW + k // 2 - N_WEIGHT_CHUNKS
                act.wait_ge(raw_full[r % RING], 16 * (r // RING + 1) + 16 * (dr // RING) * i)
                if k >= RING:
                    act.wait_ge(half_used, k - RING + 1 + dh * i)
                nc.scalar.activation(whi[:, k % RING], raw[:, r % RING, 8 * (k % 2):8 * (k % 2) + 8], ACT.Copy)\
                    .then_inc(hi_ready, 1)

            def lead(phase, n, i, body, dr=None):
                cut_hi(2 * FIRST_CHUNK[phase] + n + 3, i, 2 * body, body if dr is None else dr)

            def done(phase, n, i, body):
                act.wait_ge(half_used, 2 * FIRST_CHUNK[phase] + n + 1 + 2 * body * i)

            def std(name):
                act.wait_ge(stat_ready, SUMS.index(name) + 1)
                nc.scalar.activation(rstd[:], aux[:, 0:T], ACT.Sqrt, bias=rms_eps, scale=1.0 / DM).then_inc(std_ready, 1)

            def fill_hi(fill, shift):
                f = FILLS.index(fill)
                if READ_BEFORE[fill]:
                    act.wait_ge(half_used, READ_BEFORE[fill])
                with act.Fori(0, 4) as i:
                    for q in range(4):
                        act.wait_ge(normed, 16 * (f if f == 0 else f - 1 if f < 4 else f - 2) + q + 1 + 4 * i)
                        if shift is None:
                            nc.scalar.activation(one(ahi, 4 * i + q), yb[:, q], ACT.Copy).then_inc(ahi_ready, 1)
                        else:
                            nc.scalar.activation(one(ahi, 4 * i + q), yb[:, q], ACT.Identity, bias=col(mod[:, shift], 4 * i + q))\
                                .then_inc(ahi_ready, 1)

            def square(name, ct, i, step, source):
                s = SUMS.index(name)
                if isinstance(i, int) and ct + step * i < 2:
                    if s:
                        act.wait_ge(ssq_ready, 17 * s)
                else:
                    act.wait_ge(ssq_ready, 17 * s + ct + step * i)
                nc.scalar.activation(ft[:, ct % 2], source, ACT.Square).then_inc(sq_ready, 1)

            act.wait_ge(par_loaded, 16)
            nc.scalar.activation(crep[:], par[:, 0:KT].unsqueeze(2).to_broadcast([P, KT, 32]), ACT.Silu).then_inc(crep_ready, 1)
            act.wait_ge(x_loaded, 16)
            act.wait_ge(res_loaded, 16)
            square("x0", 0, 0, 0, x[:, 0])
            square("x0", 1, 0, 0, x[:, 1])
            with act.Fori(1, 8) as i:
                for q in range(2):
                    square("x0", q, i, 2, one(x, 2 * i + q))

            def copy_ada(n, i):
                act.wait_ge(ada_used, KT * (n + 1) + KT * i)
                if n:
                    act.wait_ge(ada_turned, n + i)
                nc.scalar.activation(ada_row[:], ada[:, :], ACT.Copy).then_inc(ada_copied, 1)

            copy_ada(0, 0)
            copy_ada(1, 0)
            std("x0")
            for k in range(3):
                cut_hi(k)
            fill_hi("h1", 0)

            for n in range(2 * LORA_CHUNKS):
                lead("lora", n, 0, 0)
                if n % 2 == 1:
                    done("lora", n, 0, 0)
                    j = n // 2
                    nc.scalar.activation(lora_x[:, j], tile_bank(j), ACT.Identity, scale=om_mu[:, j:j + 1]).then_inc(scaled, 1)
            act.wait_ge(tile_free, 1)
            nc.scalar.activation(lora_x[0:LORA, 0], lora_x[0:LORA, 0], ACT.Tanh).then_inc(lora_act, 1)
            for j in (1, 2):
                act.wait_ge(tile_free, j + 1)
                nc.scalar.activation(lora_x[:, j], lora_x[:, j], ACT.Sigmoid).then_inc(lora_act, 1)

            def lora_decay(j):
                act.wait_ge(lora_mm, j + 1)
                for w, (dst, bias) in enumerate(((mix, "w0"), (aa, "a0"))):
                    for p in range(2):
                        nc.scalar.activation(dst[:, 2 * j + p], work[2 * (j % 2) + w][:, p * T:(p + 1) * T], ACT.Sigmoid,
                                             bias=pcol(bias, 2 * j + p)).then_inc(lora_out, 1)

            def shifted_tile(j, i):
                t = FIRST_TILE["wkv"] + j
                if j < 6:
                    dst = (kraw, rraw, vraw)[j // 2][:, j % 2]
                    nc.scalar.activation(dst, tile_bank(t), ACT.Identity, scale=col(om_mu, 3 + 8 * (j // 2) + j % 2 + 2 * i))\
                        .then_inc(scaled, 1)
                else:
                    nc.scalar.activation(one(mix, NR + j - 6 + 2 * i), tile_bank(t), ACT.Copy).then_inc(tile_free, 1)

            def turned_out(g):
                for b in range(3):
                    act.wait_ge(turned, 3 * g + b + 1)
                    nc.scalar.activation(tok[:].rearrange("p a b c -> p (a b c)")[:, 512 * b:512 * b + 512], work[b][:, :], ACT.Copy)\
                        .then_inc(tok_ready, 1)

            def keys_out(g):
                act.wait_ge(av_mm, g + 1)
                nc.scalar.activation(av[:].rearrange("p a h t -> p (a h t)"), work[3][:, :], ACT.Copy).then_inc(av_ready, 1)

            def variance_in(g):
                act.wait_ge(centred, g + 1)
                nc.scalar.activation(flat(zmat[:]), flat(t2[:]), ACT.Square).then_inc(var_in, 1)

            def group_std(g):
                act.wait_ge(var_sum, g + 1)
                nc.scalar.activation(flat(zmat[:]), aux[:, :], ACT.Sqrt, bias=gn_eps, scale=1.0 / HEAD).then_inc(gn_std, 1)

            def group_affine(g):
                act.wait_ge(gn_out, 1 + g)
                for p in range(2):
                    nc.scalar.activation(t2[:, p], t2[:, p], ACT.Identity, scale=pcol("ln_w", p + 2 * g), bias=pcol("ln_b", p + 2 * g))\
                        .then_inc(normed_y, 1)

            def wkv_body(i, opening):
                g = i - 1
                for n in range(16):
                    lead("wkv", n, i, WKV_CHUNKS, WKV_RAW)
                    if n % 2 == 1:
                        done("wkv", n, i, WKV_CHUNKS)
                        j = n // 2
                        if not opening and n == 1:
                            act.wait_ge(prep_done, i)
                        if not opening and n == 9:
                            act.wait_ge(turned, 3 * i)
                        shifted_tile(j, i)
                    if opening:
                        for j in LORA_AT.get(n, ()):
                            lora_decay(j)
                    elif n == 0:
                        turned_out(g)
                    if not opening and n == 3:
                        keys_out(g)
                    if n == 2:
                        act.wait_ge(cumulated, i + 1)
                        nc.scalar.activation(flat(ep[:]), flat(en[:]), ACT.Exp, scale=-EXP_HALF).then_inc(decays, 1)
                        nc.scalar.activation(flat(ea[:]), flat(ea[:]), ACT.Exp, scale=-EXP_HALF).then_inc(decays, 1)
                        act.wait_ge(decays, 2 + 3 * i)
                        nc.scalar.activation(flat(en[:]), flat(en[:]), ACT.Exp, scale=EXP_HALF).then_inc(decays, 1)
                    if n == 5:
                        act.wait_ge(kk_raw, i + 1)
                        nc.scalar.activation(flat(t2[:]), flat(kk), ACT.Square).then_inc(kk_sq, 1)
                    if n == 6:
                        act.wait_ge(kk_sum, i + 1)
                        nc.scalar.activation(flat(t2[:]), aux[:, :], ACT.Sqrt).then_inc(kk_norm, 1)
                    if not opening:
                        if n == 12:
                            variance_in(g)
                        if n == 13:
                            group_std(g)
                        if n == 14:
                            group_affine(g)
                copy_ada(2, i)

            wkv_body(0, True)
            with act.Fori(1, NGROUP) as i:
                wkv_body(i, False)
            g = NGROUP - 1
            act.wait_ge(prep_done, NGROUP)
            act.dma_start(pool_w[:].rearrange("p g a b n -> p (g a b n)"), pool_w_in).then_inc(pool_loaded, 16)
            act.dma_start(flat(pool_inv[:]), pool_inv_in).then_inc(pool_loaded, 16)
            turned_out(g)
            keys_out(g)
            variance_in(g)
            group_std(g)
            group_affine(g)
            for j in range(NPOOL):
                act.wait_ge(pool_mm, j + 1)
                for d in range(2):
                    nc.scalar.activation(mix[:, NR + 2 * j + d], work[j][:, d * T:(d + 1) * T], ACT.Identity,
                                         scale=pcol("pool_scale", 2 * j + d), bias=pbs[:, 2 * j + d:2 * j + d + 1])\
                        .then_inc(pool_out, 1)
            act.wait_ge(mixed, NGROUP)
            act.wait_ge(pool_out, 2 * NPOOL)
            act.wait_ge(half_used, READ_BEFORE["mixed"])
            for q in range(4):
                nc.scalar.activation(ahi[:, 4 * q:4 * q + 4], mix[:, 4 * q:4 * q + 4], ACT.Copy).then_inc(ahi_ready, 4)

            def residual(phase, name):
                with act.Fori(0, 4) as i:
                    for n in range(8):
                        lead(phase, n, i, 4)
                        if n % 2 == 1:
                            residual_square(phase, name, n // 2, i)

            def residual_square(phase, name, j, i):
                act.wait_ge(tile_free, FIRST_TILE[phase] + j + 1 + 4 * i)
                s = SUMS.index(name)
                if j < 2 and isinstance(i, int) and i == 0:
                    act.wait_ge(ssq_ready, 17 * s)
                else:
                    act.wait_ge(ssq_ready, 17 * s + j + 4 * i)
                if name == "x2":
                    nc.scalar.activation(yb[:, j % 2], one(x, j + 4 * i), ACT.Square, scale=pcol("norm_f_g", j + 4 * i))
                nc.scalar.activation(ft[:, j % 2], one(x, j + 4 * i), ACT.Square).then_inc(sq_ready, 1)

            def up(phase, conv, bias, tap, which):
                def silu(p, i):
                    act.wait_ge(tile_free, FIRST_TILE[phase] + 2 * p + 2 + 4 * i)
                    nc.scalar.activation(yb[:, 2 * p + 1], yb[:, 2 * p + 1], ACT.Silu).then_inc(silu_ready, 1)

                def high(p, i):
                    act.wait_ge(gated, which * NF + p + 1 + 2 * i)
                    nc.scalar.activation(one(ffhi, p + 2 * i), ft[:, p], ACT.Copy).then_inc(ffhi_ready, 1)

                def body(i, first=False):
                    for n in range(8):
                        lead(phase, n, i, 4)
                        if n == 4:
                            silu(0, i)
                        if n == 0 and not first:
                            silu(1, i - 1)
                        if n % 2 == 1:
                            done(phase, n, i, 4)
                            j = n // 2
                            nc.scalar.activation(yb[:, j], tile_bank(FIRST_TILE[phase] + j), ACT.Identity,
                                                 scale=pcol(conv, 3 * j + tap + 12 * i), bias=pcol(bias, j + 4 * i)).then_inc(scaled, 1)
                        if n == 5:
                            high(0, i)
                        if n == 1 and not first:
                            high(1, i - 1)

                body(0, True)
                with act.Fori(1, 22) as i:
                    body(i)
                silu(1, 21)
                high(1, 21)

            def down(phase, name):
                def body(i):
                    for j in range(4):
                        for n in range(6 * j, 6 * j + 6):
                            lead(phase, n, i, 12)
                        residual_square(phase, name, j, i)
                with act.Fori(0, 3) as i:
                    body(i)
                body(3)

            residual("wout", "x1")
            std("x1")
            fill_hi("h2", 3)
            up("up1", "conv_w", "conv_b", 2, 0)
            down("down1", "x2")
            act.dma_start(catt[:], att_in).then_inc(att_loaded, 16)
            std("x2")
            act.wait_ge(second_mean, 1)
            nc.scalar.activation(wssq[:], wssq[:], ACT.Sqrt, bias=rms_eps, scale=1.0 / DM).then_inc(second_std, 1)
            fill_hi("u1", None)

            for n in range(24):
                lead("qkv", n, 0, 0)
                if n % 2 == 1:
                    done("qkv", n, 0, 0)
                    nc.scalar.activation(qkv[:, n // 2], tile_bank(FIRST_TILE["qkv"] + n // 2), ACT.Copy).then_inc(tile_free, 1)

            with act.Fori(0, 2) as i:
                for n in range(24):
                    lead("cvb", n, i, 12)
                    if n % 6 == 1:
                        done("cvb", n, i, 12)
                        nc.scalar.activation(yb[:, 0], tile_bank(FIRST_TILE["cvb"] + n // 2), ACT.Copy).then_inc(tile_free, 1)
                    if n % 6 == 5:
                        act.wait_ge(tile_free, FIRST_TILE["cvb"] + n // 2 + 1 + 12 * i)
                        nc.scalar.activation(one(yahi, n // 6 + 4 * i), ft[:, (n // 6) % 2], ACT.Copy).then_inc(yahi_ready, 1)

            act.wait_ge(vt_mm, 1)
            nc.scalar.activation(flat(vtok[:]), work[1][:, :], ACT.Copy).then_inc(vt_ready, 1)

            def attend(n, i, kv):
                j = 4 * kv + i
                if n == 2:
                    act.wait_ge(shifted, 2 * j + 1)
                    for e in range(2):
                        for b in range(2):
                            nc.scalar.activation(prob[:, e, b], prob[:, e, b], ACT.Exp, bias=small[:, 4 + 2 * e + b:5 + 2 * e + b],
                                                 accum_out=small[:, 12 + 2 * e + b:13 + 2 * e + b]).then_inc(expd, 1)
                    act.wait_ge(shifted, 2 * j + 2)
                    nc.scalar.activation(small[:, 8:12], small[:, 8:12], ACT.Exp).then_inc(expd, 1)
                if n == 4:
                    for e in range(2):
                        act.wait_ge(pt_mm, 2 * j + e + 1)
                        if e == 0:
                            if not isinstance(j, int) or j:
                                act.wait_ge(o_mm, j)
                        nc.scalar.activation(flat(pt[:, 2 * e:2 * e + 2]), work[1 + e][:, :], ACT.Copy).then_inc(pt_ready, 1)
                if n == 6:
                    act.wait_ge(o_mm, j + 1)
                    nc.scalar.activation(one(oahi, j), work[3][:, 0:T], ACT.Copy).then_inc(oahi_ready, 1)

            for kv in range(2):
                def body(i, kv=kv):
                    for n in range(8):
                        cut_hi(2 * FIRST_CHUNK["gates"] + 32 * kv + n + 3, i, 8, 4)
                        if n % 2 == 1:
                            act.wait_ge(half_used, 2 * FIRST_CHUNK["gates"] + 32 * kv + n + 1 + 8 * i)
                            j = 16 * kv + n // 2
                            nc.scalar.activation(one(gates, j + 4 * i), tile_bank(FIRST_TILE["gates"] + j), ACT.Sigmoid,
                                                 bias=pcol("b_gate", j + 4 * i)).then_inc(tile_free, 1)
                        attend(n, i, kv)
                if kv == 0:
                    body(0)
                with act.Fori(1 - kv, 4) as i:
                    body(i)

            act.wait_ge(half_used, READ_BEFORE["gmix"])
            with act.Fori(0, 4) as i:
                for n in range(8):
                    lead("ao", n, i, 4)
                    if n % 2 == 1:
                        act.wait_ge(merged, n // 2 + 1 + 4 * i)
                        nc.scalar.activation(one(ahi, n // 2 + 4 * i), ft[:, (n // 2) % 2], ACT.Copy).then_inc(ahi_ready, 1)
            residual("mix", "x4")
            std("x4")
            fill_hi("u2", None)
            up("up2", "conv2_w", "conv2_b", 1, 1)
            down("down2", "x5")
            std("x5")

        @block.vector
        def _(dve):
            link, enter, leave = make_chain(dve, dve_chain)

            def cut_lo(k, i=0, dh=0, dr=0):
                if isinstance(i, int) and k + dh * i >= 2 * N_WEIGHT_CHUNKS:
                    return
                r = RAW[k // 2] if k // 2 < N_WEIGHT_CHUNKS else N_RAW + k // 2 - N_WEIGHT_CHUNKS
                dve.wait_ge(hi_ready, k + 1 + dh * i)
                nc.vector.tensor_tensor(wlo[:, k % RING], raw[:, r % RING, 8 * (k % 2):8 * (k % 2) + 8],
                                        whi[:, k % RING].bitcast(F32), ALU.subtract).then_inc(lo_ready, 1)

            def lead(phase, n, i, body, dr=None):
                cut_lo(2 * FIRST_CHUNK[phase] + n + 2, i, 2 * body, body if dr is None else dr)

            def done(phase, n, i, body):
                dve.wait_ge(half_used, 2 * FIRST_CHUNK[phase] + n + 1 + 2 * body * i)

            def reciprocal_std(name):
                dve.wait_ge(std_ready, SUMS.index(name) + 1)
                link(nc.vector.reciprocal(rstd[:], rstd[:]))

            def fill_lo(fill, scale, shift, rstd=rstd):
                f = FILLS.index(fill)
                u = f if f == 0 else f - 1 if f < 4 else f - 2

                def normed_tile(q, i):
                    if not (isinstance(i, int) and i == 0):
                        dve.wait_ge(a_ready, 16 * f + q + 1 + 4 * i - 4)
                    nc.vector.scalar_tensor_tensor(out=yb[:, q], in0=one(x, q + 4 * i), scalar=scale(q + 4 * i), in1=rstd[:],
                                                   op0=ALU.mult, op1=ALU.mult).then_inc(normed, 1)

                def low_tile(q, i):
                    dve.wait_ge(normed, 16 * u + q + 1 + 4 * i)
                    dve.wait_ge(ahi_ready, 16 * f + q + 1 + 4 * i)
                    nc.vector.scalar_tensor_tensor(out=one(alo, q + 4 * i), in0=yb[:, q],
                                                   scalar=0.0 if shift is None else col(mod[:, shift], q + 4 * i),
                                                   in1=one(ahi, q + 4 * i).bitcast(F32), op0=ALU.add, op1=ALU.subtract)\
                        .then_inc(a_ready, 1)

                def four(i):
                    normed_tile(0, i)
                    normed_tile(1, i)
                    for q in range(4):
                        if q < 2:
                            normed_tile(q + 2, i)
                        low_tile(q, i)

                four(0)
                with dve.Fori(1, 4) as i:
                    four(i)

            dve.wait_ge(par_loaded, 16)
            nc.vector.tensor_scalar(om_mu[:], pcol("mu", 0, 27), -1.0, 1.0, ALU.mult, ALU.add).then_inc(derived, 1)
            nc.vector.tensor_scalar(om_ka[:], pcol("k_a", 0, NR), -1.0, 1.0, ALU.mult, ALU.add).then_inc(derived, 1)
            nc.vector.tensor_tensor(pbs[:], pcol("pool_b", 0, NR), pcol("pool_scale", 0, NR), ALU.mult).then_inc(derived, 1)
            dve.wait_ge(derived, 3)

            def mod_columns(n, i):
                dve.wait_ge(ada_turned, n + 1 + i)
                src = aux[:, :].rearrange("p (b g r) -> p g b r", b=4, g=4)[:, :, :, 0]
                if isinstance(i, int):
                    dst = mod[:, n + i].rearrange("p (g b) -> p g b", g=4)
                    bias = pcol("b_ada", KT * (n + i), KT).rearrange("p (g b) -> p g b", g=4)
                else:
                    dst = mod[:, bass.ds(n + i, 1)].rearrange("p o (g b) -> p (o g) b", g=4)
                    bias = pcol("b_ada", KT * n + KT * i, KT).rearrange("p (g b) -> p g b", g=4)
                nc.vector.tensor_tensor(dst, src, bias, ALU.add).then_inc(mod_ready, 1)

            def norm_scale(n, which, name):
                dve.wait_ge(mod_ready, which + 1)
                link(nc.vector.scalar_tensor_tensor(out=gs[:, n], in0=mod[:, which], scalar=1.0, in1=pcol(name, 0, KT),
                                                    op0=ALU.add, op1=ALU.mult))

            mod_columns(0, 0)
            mod_columns(1, 0)
            norm_scale(0, 1, "norm1_g")
            reciprocal_std("x0")
            cut_lo(0)
            cut_lo(1)
            fill_lo("h1", lambda n: col(gs[:, 0], n), 0)

            def token_shift(dst, t, mu):
                nc.vector.scalar_tensor_tensor(out=dst[:, 1:T], in0=tile_bank(t)[:, 0:T - 1], scalar=mu, in1=dst[:, 1:T],
                                               op0=ALU.mult, op1=ALU.add).then_inc(tile_free, 1)

            for n in range(2 * LORA_CHUNKS):
                lead("lora", n, 0, 0)
                if n % 2 == 1:
                    dve.wait_ge(scaled, n // 2 + 1)
                    token_shift(lora_x[:, n // 2], n // 2, pcol("mu", n // 2))

            def preparation(n, i):
                if n == 1:
                    if isinstance(i, int):
                        dve.wait_ge(lora_out, 4)
                        dve.wait_ge(wkv_loaded, 16)
                    for p in range(2):
                        ins = nc.vector.tensor_tensor_scan(en[:, p], scanmask, one(mix, p + 2 * i), 0.0, ALU.mult, ALU.add)
                        link(ins)
                    nc.vector.tensor_tensor(ea[:], en[:], kept(mix, 2 * i), ALU.subtract).then_inc(cumulated, 1)
                if n == 4:
                    dve.wait_ge(tile_free, FIRST_TILE["wkv"] + 2 + 8 * i)
                    nc.vector.tensor_scalar(kk[:, 0], kraw[:, 0], pcol("k_k", 2 * i), None, ALU.mult).then_inc(kk_half, 1)
                    dve.wait_ge(kk_half, i + 1)
                    nc.vector.tensor_scalar(kk[:, 1], kraw[:, 1], pcol("k_k", 2 * i + 1), None, ALU.mult).then_inc(kk_raw, 1)
                if n == 7:
                    dve.wait_ge(kk_norm, i + 1)
                    link(nc.vector.tensor_scalar(t2[:], t2[:], L2_EPS, None, ALU.max))
                    link(nc.vector.reciprocal(t2[:], t2[:]))
                    link(nc.vector.tensor_tensor(kk, kk, t2[:], ALU.mult))
                if n == 8:
                    if isinstance(i, int):
                        dve.wait_ge(lora_out, 16)
                    for p in range(2):
                        link(nc.vector.tensor_scalar(t1[:, p], one(aa, p + 2 * i), pcol("k_a", p + 2 * i), col(om_ka, p + 2 * i),
                                                     ALU.mult, ALU.add))
                    link(nc.vector.tensor_tensor(t1, t1, kraw[:], ALU.mult))
                if n == 9:
                    dve.wait_ge(decays, 3 * i + 3)
                    link(nc.vector.tensor_tensor(bk[:, :, 1], t1, en[:], ALU.mult))
                    link(nc.vector.tensor_tensor(bk[:, :, 0], kk, kept(aa, 2 * i), ALU.mult))
                    link(nc.vector.tensor_tensor(bk[:, :, 0], bk[:, :, 0], en[:], ALU.mult))
                if n == 10:
                    link(nc.vector.scalar_tensor_tensor(out=t1[:, 0], in0=rraw[:, 0], scalar=pcol("r_k", 2 * i), in1=t1[:, 0],
                                                        op0=ALU.mult, op1=ALU.mult))
                    nc.vector.scalar_tensor_tensor(out=t1[:, 1], in0=rraw[:, 1], scalar=pcol("r_k", 2 * i + 1), in1=t1[:, 1],
                                                   op0=ALU.mult, op1=ALU.mult).then_inc(bonus_in, 1)
                if n == 14:
                    chunks = "p a (c t) -> p (a c) t"
                    arv = ar[:].rearrange("p a c w t -> p (a c) w t")
                    link(nc.vector.tensor_tensor(arv[:, :, 1], rraw[:].rearrange(chunks, c=4), ep[:].rearrange(chunks, c=4), ALU.mult))
                    link(nc.vector.scalar_tensor_tensor(out=arv[:, :, 0], in0=kk.rearrange(chunks, c=4), scalar=-1.0,
                                                        in1=ea[:].rearrange(chunks, c=4), op0=ALU.mult, op1=ALU.mult))
                    link(nc.vector.tensor_copy(dc[:].rearrange("p a c -> p (a c)"), ep[:].rearrange(chunks, c=4)[:, :, CH - 1]))
                if n == 15:
                    dve.wait_ge(bonus_sum, i + 1)
                    dve.wait_ge(tile_free, FIRST_TILE["wkv"] + 6 + 8 * i)
                    nc.vector.tensor_tensor(bv, aux[:, :].rearrange("p (a t) -> p a t", a=2), vraw[:], ALU.mult).then_inc(prep_done, 1)

            def masked_products(g):
                for b in range(4):
                    dve.wait_ge(products, 4 * g + b + 1)
                    nc.vector.tensor_tensor(nb[:, 2 * b:2 * b + 2].rearrange("p m w t -> p m (w t)"),
                                            work[b][:, :].rearrange("p (m x) -> p m x", m=2),
                                            prodmask.unsqueeze(1).to_broadcast([P, 2, 256]), ALU.mult).then_inc(products_masked, 1)

            eyes = eye.unsqueeze(1).to_broadcast([P, 8, CH])

            def mats(b):
                return b[:, :].rearrange("p (m t) -> p m t", m=8)

            def level_start(g):
                dve.wait_ge(level_ready, 6 * g + 1)
                link(nc.vector.tensor_tensor(tinv[:], bm[:, 0], eyes, ALU.add))
                dve.wait_ge(level_z, 6 * g + 1)
                nc.vector.tensor_tensor(tinvt[:], mats(work[3]), eyes, ALU.add).then_inc(level_done, 1)

            def level_copy(g, level):
                dve.wait_ge(level_z, 6 * g + level + 1)
                nc.vector.tensor_copy(zmat[:], mats(work[0])).then_inc(level_zs, 1)

            def level_add(g, level):
                dve.wait_ge(level_t, 9 * g + 2 * level - 1)
                if level < 5:
                    nc.vector.tensor_tensor(tinvt[:], tinvt[:], mats(work[2]), ALU.add).then_inc(level_done, 1)
                    dve.wait_ge(level_t, 9 * g + 2 * level)
                    link(nc.vector.tensor_tensor(tinv[:], tinv[:], mats(work[1]), ALU.add))
                else:
                    nc.vector.tensor_tensor(tinv[:], tinv[:], mats(work[1]), ALU.add).then_inc(level_done, 1)

            def r_out(g, c):
                e = 64 * (c % 2)
                dve.wait_ge(r_mm, 4 * g + c + 1)
                if c == 0:
                    dve.wait_ge(av_ready, g + 1)
                nc.vector.tensor_tensor(rs[e:e + 64], work[0][e:e + 64, 0:256].rearrange("p (h t) -> p h t", h=4),
                                        av[e:e + 64, c // 2], ALU.add).then_inc(r_ready, 1)

            def u_out(g, c):
                e = 64 * (c % 2)
                dve.wait_ge(u_mm, 4 * g + c + 1)
                nc.vector.tensor_copy(us[e:e + 64].rearrange("p h t -> p (h t)"), work[1][e:e + 64, 0:256]).then_inc(u_ready, 1)

            def s_out(g, c):
                dve.wait_ge(s_mm, 3 * g + c + 1)
                for p in range(2):
                    ins = nc.vector.scalar_tensor_tensor(out=state[:, (c + 1) % 2, p], in0=work[2][:, p * P:(p + 1) * P],
                                                         scalar=dc[:, p, c:c + 1], in1=headones, op0=ALU.mult, op1=ALU.mult)
                ins.then_inc(s_ready, 1)

            def y_out(g):
                dve.wait_ge(y_mm, 4 * g + 4)
                nc.vector.tensor_copy(flat(t2[:]), work[3][:, :]).then_inc(y_ready, 1)

            def centre(g):
                dve.wait_ge(mean_sum, g + 1)
                nc.vector.scalar_tensor_tensor(out=flat(t2[:]), in0=aux[:, :], scalar=-1.0 / HEAD, in1=flat(t2[:]), op0=ALU.mult,
                                               op1=ALU.add).then_inc(centred, 1)

            def normalise(g):
                dve.wait_ge(gn_std, g + 1)
                link(nc.vector.reciprocal(zmat[:], zmat[:]))
                nc.vector.tensor_tensor(flat(t2[:]), flat(t2[:]), flat(zmat[:]), ALU.mult).then_inc(gn_out, 1)

            def finish_group(g):
                dve.wait_ge(normed_y, 2 * g + 2)
                link(nc.vector.tensor_tensor(t2[:], t2[:], bv, ALU.add))
                nc.vector.tensor_tensor(kept(mix, 2 * g), t2[:], kept(g_sb, 2 * g), ALU.mult).then_inc(mixed, 1)

            def recurrence(n, g):
                if n == 0:
                    masked_products(g)
                if n == 1:
                    level_start(g)
                    level_copy(g, 1)
                if 2 <= n <= 6:
                    level_add(g, n - 1)
                    if n < 6:
                        level_copy(g, n)
                    else:
                        r_out(g, 0)
                if n == 7:
                    u_out(g, 0)
                    s_out(g, 0)
                if n == 8:
                    r_out(g, 1)
                    u_out(g, 1)
                if n == 9:
                    s_out(g, 1)
                    r_out(g, 2)
                if n == 10:
                    u_out(g, 2)
                    s_out(g, 2)
                if n == 11:
                    r_out(g, 3)
                    u_out(g, 3)
                if n == 12:
                    y_out(g)
                    centre(g)
                if n == 13:
                    normalise(g)
                if n == 14:
                    finish_group(g)

            def wkv_body(i, opening):
                for n in range(16):
                    lead("wkv", n, i, WKV_CHUNKS, WKV_RAW)
                    if n % 2 == 1 and n // 2 < 6:
                        j = n // 2
                        dve.wait_ge(scaled, SCALED["wkv"] + j + 1 + 6 * i)
                        token_shift((kraw, rraw, vraw)[j // 2][:, j % 2], FIRST_TILE["wkv"] + j, pcol("mu", 3 + 8 * (j // 2) + j % 2 + 2 * i))
                    if opening:
                        if 5 <= n <= 8:
                            j = n - 5
                            dve.wait_ge(lora_mm, 5 + j)
                            link(nc.vector.tensor_copy(flat(g_sb[:, 2 * j:2 * j + 2]), work[j][:, :]))
                    else:
                        recurrence(n, i - 1)
                    preparation(n, i)
                mod_columns(2, i)

            wkv_body(0, True)
            with dve.Fori(1, NGROUP) as i:
                enter(i, 1, WKV_LINKS)
                wkv_body(i, False)
                leave(1, NGROUP - 1)
            for n in range(16):
                recurrence(n, NGROUP - 1)
            norm_scale(1, 4, "norm2_g")
            for q in range(4):
                dve.wait_ge(mixed, NGROUP)
                dve.wait_ge(ahi_ready, 16 * FILLS.index("mixed") + 4 * q + 4)
                nc.vector.tensor_tensor(alo[:, 4 * q:4 * q + 4], mix[:, 4 * q:4 * q + 4], ahi[:, 4 * q:4 * q + 4].bitcast(F32),
                                        ALU.subtract).then_inc(a_ready, 4)

            def residual_tile(phase, j, i, scale):
                t = FIRST_TILE[phase] + j
                dst = one(x, j + 4 * i)
                if scale is None:
                    ins = nc.vector.tensor_tensor(dst, tile_bank(t), dst, ALU.add)
                else:
                    ins = nc.vector.scalar_tensor_tensor(out=dst, in0=tile_bank(t), scalar=col(mod[:, scale], j + 4 * i), in1=dst,
                                                         op0=ALU.mult, op1=ALU.add)
                ins.then_inc(tile_free, 1)

            def residual(phase, scale):
                with dve.Fori(0, 4) as i:
                    for n in range(8):
                        lead(phase, n, i, 4)
                        if n % 2 == 1:
                            done(phase, n, i, 4)
                            residual_tile(phase, n // 2, i, scale)

            def up(phase, conv, taps, which):
                def gate(p, i):
                    dve.wait_ge(silu_ready, which * NF + p + 1 + 2 * i)
                    nc.vector.tensor_tensor(ft[:, p], yb[:, 2 * p + 1], yb[:, 2 * p], ALU.mult).then_inc(gated, 1)

                def low(p, i):
                    dve.wait_ge(ffhi_ready, which * NF + p + 1 + 2 * i)
                    nc.vector.tensor_tensor(one(fflo, p + 2 * i), ft[:, p], one(ffhi, p + 2 * i).bitcast(F32),
                                            ALU.subtract).then_inc(ff_ready, 1)

                def body(i, first=False):
                    for n in range(8):
                        lead(phase, n, i, 4)
                        if n == 5:
                            gate(0, i)
                        if n == 1 and not first:
                            gate(1, i - 1)
                        if n == 6:
                            low(0, i)
                        if n == 2 and not first:
                            low(1, i - 1)
                        if n % 2 == 0:
                            continue
                        j = n // 2
                        dve.wait_ge(scaled, SCALED[phase] + j + 1 + 4 * i)
                        u = tile_bank(FIRST_TILE[phase] + j)
                        for m, (tap, back) in enumerate(taps):
                            dst, src = (slice(back, T), slice(0, T - back)) if back > 0 else (slice(0, T + back), slice(-back, T))
                            ins = nc.vector.scalar_tensor_tensor(out=yb[:, j, dst], in0=u[:, src],
                                                                 scalar=pcol(conv, 3 * j + tap + 12 * i), in1=yb[:, j, dst],
                                                                 op0=ALU.mult, op1=ALU.add)
                            if m == 0:
                                link(ins)
                        ins.then_inc(tile_free, 1)

                body(0, True)
                with dve.Fori(1, 22) as i:
                    enter(i, 1, 4)
                    body(i)
                    leave(1, 21)
                gate(1, 21)
                low(1, 21)

            def down(phase, scale):
                def body(i):
                    for j in range(4):
                        for n in range(6 * j, 6 * j + 6):
                            lead(phase, n, i, 12)
                        done(phase, 6 * j + 5, i, 12)
                        residual_tile(phase, j, i, scale)
                with dve.Fori(0, 3) as i:
                    body(i)
                body(3)

            def scaled_x(name):
                for kt in range(KT):
                    nc.vector.scalar_tensor_tensor(out=x[:, kt], in0=x[:, kt], scalar=pcol(name, kt), in1=rstd[:],
                                                   op0=ALU.mult, op1=ALU.mult).then_inc(xnew, 1)

            residual("wout", 2)
            reciprocal_std("x1")
            fill_lo("h2", lambda n: col(gs[:, 1], n), 3)
            up("up1", "conv_w", ((1, 1), (0, 2)), 0)
            down("down1", 5)
            reciprocal_std("x2")
            link(nc.vector.tensor_tensor(wssq[:], aux[:, T:2 * T], rstd[:], ALU.mult))
            nc.vector.tensor_tensor(wssq[:], wssq[:], rstd[:], ALU.mult).then_inc(second_mean, 1)
            scaled_x("norm_f_g")
            dve.wait_ge(second_std, 1)
            link(nc.vector.reciprocal(wssq[:], wssq[:]))
            dve.wait_ge(xnew, KT)
            fill_lo("u1", lambda n: pcol("norm_mix_g", n), None, wssq)
            for n in range(24):
                lead("qkv", n, 0, 0)

            with dve.Fori(0, 2) as i:
                enter(i, 0, 8)
                for n in range(24):
                    lead("cvb", n, i, 12)
                    j = n // 6
                    if n % 6 == 3:
                        done("cvb", n, i, 12)
                        dve.wait_ge(tile_free, FIRST_TILE["cvb"] + n // 2 + 12 * i)
                        nc.vector.tensor_tensor(yb[:, 1], tile_bank(FIRST_TILE["cvb"] + n // 2), yb[:, 0], ALU.mult)\
                            .then_inc(tile_free, 1)
                        dve.wait_ge(tile_free, FIRST_TILE["cvb"] + n // 2 + 1 + 12 * i)
                        cvj = 3 * j + 12 * i
                        link(nc.vector.tensor_scalar(yb[:, 2], yb[:, 1], pcol("conv_a_w", cvj + 1), None, ALU.mult))
                        link(nc.vector.scalar_tensor_tensor(out=yb[:, 2, 1:T], in0=yb[:, 1, 0:T - 1], scalar=pcol("conv_a_w", cvj),
                                                            in1=yb[:, 2, 1:T], op0=ALU.mult, op1=ALU.add))
                        nc.vector.scalar_tensor_tensor(out=yb[:, 2, 0:T - 1], in0=yb[:, 1, 1:T], scalar=pcol("conv_a_w", cvj + 2),
                                                       in1=yb[:, 2, 0:T - 1], op0=ALU.mult, op1=ALU.add).then_inc(convolved, 1)
                    if n % 6 == 5:
                        done("cvb", n, i, 12)
                        dve.wait_ge(convolved, j + 1 + 4 * i)
                        nc.vector.tensor_tensor(ft[:, j % 2], tile_bank(FIRST_TILE["cvb"] + n // 2), yb[:, 2], ALU.mult)\
                            .then_inc(tile_free, 1)
                        dve.wait_ge(yahi_ready, j + 1 + 4 * i)
                        nc.vector.tensor_tensor(one(yalo, j + 4 * i), ft[:, j % 2], one(yahi, j + 4 * i).bitcast(F32), ALU.subtract)\
                            .then_inc(ya_ready, 1)
                leave(0, 2)

            def rope(dst, src, turned_bank):
                link(nc.vector.tensor_tensor(turned_rot, turned_bank, sin, ALU.mult))
                link(nc.vector.tensor_tensor(dst, src, cos, ALU.mult))
                nc.vector.tensor_tensor(dst, dst, turned_rot, ALU.add).then_inc(roped, 1)

            turned_rot = ft[:, 0]
            dve.wait_ge(att_loaded, 16)
            for p in range(2):
                dve.wait_ge(rot_mm, 1)
                if p:
                    dve.wait_ge(roped, p)
                rope(qkv[:, 8 + p], qkv[:, 8 + p], work[0][:, p * T:(p + 1) * T])
            dve.wait_ge(roped, 2)

            def attend(n, i, kv):
                j = 4 * kv + i
                if n == 0:
                    dve.wait_ge(rot_mm, j + 2)
                    if not isinstance(j, int) or j:
                        dve.wait_ge(score_mm, 2 * j)
                    dve.wait_ge(roped, j + 2)
                    rope(qr[:], one(qkv, 4 * kv + i), work[0][:, 0:T])
                if n == 1:
                    for e in range(2):
                        dve.wait_ge(score_mm, 2 * j + e + 1)
                        if e == 0 and (not isinstance(j, int) or j):
                            dve.wait_ge(pt_mm, 2 * j)
                        nc.vector.scalar_tensor_tensor(out=flat(prob[:, e]), in0=work[1 + e][:, :], scalar=HEAD ** -0.5, in1=band,
                                                       op0=ALU.mult, op1=ALU.add).then_inc(masked, 1)
                    dve.wait_ge(masked, 2 * j + 2)
                    link(nc.vector.tensor_reduce(small[:, 0:4], prob[:].rearrange("p e b s -> p (e b) s"), AX.X, ALU.max))
                    sink = pcol("sink", 8 * kv + 2 * i, 2).unsqueeze(2).to_broadcast([P, 2, 2])
                    m = small[:, 0:4].rearrange("p (e b) -> p e b", e=2)
                    link(nc.vector.tensor_tensor(m, m, sink, ALU.max))
                    nc.vector.tensor_scalar(small[:, 4:8], small[:, 0:4], -1.0, None, ALU.mult).then_inc(shifted, 1)
                    nc.vector.tensor_tensor(small[:, 8:12].rearrange("p (e b) -> p e b", e=2), sink, m, ALU.subtract).then_inc(shifted, 1)
                if n == 3:
                    dve.wait_ge(expd, 5 * j + 5)
                    link(nc.vector.tensor_tensor(small[:, 12:16], small[:, 12:16], small[:, 8:12], ALU.add))
                    link(nc.vector.reciprocal(small[:, 12:16], small[:, 12:16]))
                    for m in range(4):
                        ins = nc.vector.tensor_scalar(prob[:, m // 2, m % 2], prob[:, m // 2, m % 2], small[:, 12 + m:13 + m], None,
                                                      ALU.mult)
                        if m < 3:
                            link(ins)
                    ins.then_inc(divided, 1)
                if n == 6:
                    dve.wait_ge(oahi_ready, j + 1)
                    nc.vector.tensor_tensor(one(oalo, j), work[3][:, 0:T], one(oahi, j).bitcast(F32), ALU.subtract).then_inc(oa_ready, 1)

            for kv in range(2):
                def body(i, kv=kv):
                    for n in range(8):
                        cut_lo(2 * FIRST_CHUNK["gates"] + 32 * kv + n + 2, i, 8, 4)
                        attend(n, i, kv)
                if kv == 0:
                    body(0)
                with dve.Fori(1 - kv, 4) as i:
                    enter(i, 1 - kv, 9)
                    body(i)
                    leave(1 - kv, 3 + kv)

            dve.wait_ge(tile_free, FIRST_TILE["ao"])
            with dve.Fori(0, 4) as i:
                for n in range(8):
                    lead("ao", n, i, 4)
                    done("ao", n, i, 4)
                    t = FIRST_TILE["ao"] + n
                    ct = n // 2 + 4 * i
                    part = (n // 2) % 2
                    nc.vector.tensor_tensor(yb[:, 2 * part + n % 2], tile_bank(t), one(gates, ct + KT * (n % 2)), ALU.mult)\
                        .then_inc(tile_free, 1)
                    if n % 2 == 1:
                        dve.wait_ge(tile_free, t + 1 + 8 * i)
                        nc.vector.tensor_tensor(ft[:, part], yb[:, 2 * part], yb[:, 2 * part + 1], ALU.add).then_inc(merged, 1)
                        dve.wait_ge(ahi_ready, 16 * FILLS.index("gmix") + n // 2 + 1 + 4 * i)
                        nc.vector.tensor_tensor(one(alo, ct), ft[:, part], one(ahi, ct).bitcast(F32), ALU.subtract).then_inc(a_ready, 1)

            residual("mix", None)
            reciprocal_std("x4")
            fill_lo("u2", lambda n: pcol("norm_ffn_g", n), None)
            up("up2", "conv2_w", ((0, 1), (2, -1)), 1)
            down("down2", None)
            reciprocal_std("x5")
            scaled_x("norm_final_g")

        @block.gpsimd
        def _(pool):
            link, enter, leave = make_chain(pool, pool_chain)

            def sum_squares(name):
                s = SUMS.index(name)
                if s:
                    pool.wait_ge(stat_ready, s)
                if name == "x2":
                    link(nc.gpsimd.memset(wssq[:], 0.0))
                nc.gpsimd.memset(ssq[:], 0.0).then_inc(ssq_ready, 1)
                with pool.Fori(0, 8) as i:
                    enter(i, 0, 2 if name == "x2" else 0)
                    for q in range(2):
                        pool.wait_ge(sq_ready, 16 * s + q + 1 + 2 * i)
                        if name == "x2":
                            link(nc.gpsimd.tensor_tensor(wssq[:], wssq[:], yb[:, q], ALU.add))
                        pool.wait_ge(ssq_ready, 17 * s + q + 1 + 2 * i)
                        nc.gpsimd.tensor_tensor(ssq[:], ssq[:], ft[:, q], ALU.add).then_inc(ssq_ready, 1)
                    leave(0, 8)

            sum_squares("x0")

            def levels(g):
                if not isinstance(g, int) or g:
                    pool.wait_ge(y_mm, 4 * g)
                    pool.sem_inc(pool_held, 1)
                nc.gpsimd.memset(state[:, 0], 0.0).then_inc(state_zero, 1)
                pool.wait_ge(products_masked, 4 * g + 4)
                for level in range(6):
                    if level >= 2:
                        pool.wait_ge(level_z, 6 * g + level - 1)
                        pool.wait_ge(level_done, 6 * g + level - 1)
                    mask = cw[:, 256 + CH * level:256 + CH * (level + 1)].unsqueeze(1).to_broadcast([P, 8, CH])
                    nc.gpsimd.tensor_tensor(bm[:, level % 2], nb[:, :, 0], mask, ALU.mult).then_inc(level_ready, 1)

            levels(0)
            with pool.Fori(1, NGROUP) as i:
                levels(i)

            pool.wait_ge(pool_loaded, 32)
            pool.wait_ge(tile_free, FIRST_TILE["wout"])
            link(nc.gpsimd.memset(pad_a[:, :, 0:16], 0.0))
            link(nc.gpsimd.memset(pad_b[:, :, 0:16], 0.0))
            for j in range(NPOOL):
                u = mix[:, NR + 2 * j:NR + 2 * j + 2]
                link(nc.gpsimd.tensor_copy(pad_a[:, :, 16:16 + T], u))
                src, dst = pad_a, pad_b
                for level in range(j + 1):
                    step = 1 << level
                    link(nc.gpsimd.tensor_tensor(dst[:, :, 16:16 + T], src[:, :, 16:16 + T], src[:, :, 16 - step:16 + T - step], ALU.add))
                    src, dst = dst, src
                link(nc.gpsimd.tensor_tensor(dst[:, :, 16:16 + T], src[:, :, 16:16 + T],
                                             pool_inv[:, j].unsqueeze(1).to_broadcast([P, 2, T]), ALU.mult))
                nc.gpsimd.tensor_tensor(u, dst[:, :, 16:16 + T], u, ALU.subtract).then_inc(pool_z, 1)
                pool.wait_ge(pool_z, j + 1)

            for name in ("x1", "x2", "x4", "x5"):
                sum_squares(name)
            pool.wait_ge(xnew, 2 * KT)
            pool.dma_start(out, x[:]).then_inc(out_stored, 16)


def build(nc, args):
    blocks_program(nc, *args)


def _columns(v):
    import numpy as np
    return np.ascontiguousarray(v.reshape(-1, 128).T)


def _chunks(w):
    k, n = w.shape
    return w.reshape(k // 128, 128, n // 128, 128).transpose(2, 1, 0, 3).reshape(n // 128, 128, k)


def _down_chunks(w):
    import numpy as np
    k, n = w.shape
    t = w.reshape(k // 128, 128, n // 128, 128).transpose(2, 1, 0, 3)
    out = np.zeros((n // 128, 3, 128, 16, 128), w.dtype)
    for c in range(3):
        part = t[:, :, DKT * c:DKT * c + DKT]
        m = part.shape[2]
        out[:, c, :, 0:min(m, 8)] = part[:, :, 0:8]
        out[:, c, :, 8:8 + m - 8] = part[:, :, 8:m]
    return out.reshape(3 * n // 128, 128, 2048)


def _interleave(a, b):
    import numpy as np
    return np.stack([a, b], 1).reshape(-1, *a.shape[1:])


def _constants():
    import numpy as np
    f = np.float32
    p, j = np.arange(128)[:, None], np.arange(128)[None]
    res = np.concatenate([np.eye(128), np.ones((128, 128)), p // 64 == j // 64, np.full((128, 1), RMS_EPS),
                          np.full((128, 1), GN_EPS)], 1).astype(f)
    s, t = np.arange(128)[:, None] % 64, np.arange(64)[None]
    strict, upper = s < t, s <= t
    levels = [(s // (2 * m) == t // (2 * m)) & (s // m % 2 == 0) & (t // m % 2 == 1) for m in (1, 2, 4, 8, 16, 32)]
    scan = np.broadcast_to(np.arange(256)[None] % CH != 0, (128, 256))
    wkv = np.concatenate([strict, upper, strict, upper, *levels, s == t, scan], 1).astype(f)
    half = HEAD // 2
    freq = f(10000.0) ** (-np.arange(half, dtype=f) / f(half))
    ang = (np.arange(256, dtype=f)[None] * freq[:, None].astype(f)).astype(f)
    cos, sin = np.tile(np.cos(ang), (4, 1)), np.tile(np.sin(ang), (4, 1))
    rot = np.zeros((128, 128))
    for c in range(128):
        rot[c + half if c % 64 < half else c - half, c] = -1.0 if c % 64 < half else 1.0
    band = np.stack([np.where(np.abs(np.arange(256)[None] - (np.arange(128)[:, None] + 128 * b)) <= 128, 0.0, MASKED)
                     for b in range(2)], 1).reshape(128, 512)
    att = np.concatenate([cos, sin, rot, band], 1).astype(f)
    inv = np.stack([1.0 / np.minimum(np.arange(1, 257), w) for w in (2, 4, 8, 16)], 0).reshape(1, -1)
    return res, wkv, att, np.broadcast_to(inv, (128, inv.shape[1])).astype(f)


def kernel(**inputs):
    import numpy as np
    import concourse.bacc as _bacc
    from concourse.bass_utils import run_bass_kernel_spmd as _run

    a = {k: np.asarray(v) for k, v in inputs.items()}
    f = np.float32
    w_in, w_in2 = a["w_in"][0], a["w_in_2"][0]
    low = 3 * DR
    pooled = low + 2 * LORA + GATE
    lora = np.zeros((DM, 3 * 128), f)
    lora[:, :2 * LORA + GATE] = w_in[:, low:pooled]
    r8, k8, v8, p8 = (_chunks(w_in[:, s:s + DR]) for s in (0, DR, 2 * DR, pooled))
    ada = a["w_ada"][0].reshape(KT, 128, 6, DM).transpose(2, 0, 1, 3).reshape(6 * KT, 128, DM)
    order = [h for j in range(NR) for h in ((j, j + 4) if j < 4 else (j + 4, j + 8))]
    cols = np.concatenate([np.arange(64 * h, 64 * h + 64) for h in order])
    q0 = 3 * DR
    q8 = _chunks(w_in2[:, q0:q0 + DR][:, cols])
    kv4 = _chunks(w_in2[:, q0 + DR:q0 + DR + 512])
    b8, c8, va8 = (_chunks(w_in2[:, s:s + DR]) for s in (0, DR, 2 * DR))
    gates = _chunks(w_in2[:, q0 + DR + 512:])
    up1, up2 = _chunks(a["w_up"][0]), _chunks(a["ffn_w_up_2"][0])
    wa = _chunks(np.concatenate([a["w_out_a_2"][0], a["w_o_attn_2"][0][cols]], 0))

    stream = np.empty((N_RAW, 128, CHUNK), f)
    stream[:ADA0] = ada[:ADA0]
    weights = [_chunks(lora)]
    for g in range(NGROUP):
        for m in (k8, r8, v8, p8):
            weights.append(m[2 * g:2 * g + 2])
    weights += [_chunks(a["w_out"][0]), _interleave(up1[:NF], up1[NF:]), _down_chunks(a["w_down"][0]), q8, kv4]
    weights += [np.stack([c8, va8, b8], 1).reshape(24, 128, CHUNK), gates, wa, _chunks(a["w_mix_out_2"][0])]
    weights += [_interleave(up2[NF:], up2[:NF]), _down_chunks(a["ffn_w_down_2"][0])]
    at = 0
    taken = np.zeros(N_RAW, bool)
    taken[:ADA0] = True
    for m in weights:
        for c in m:
            stream[RAW[at]] = c
            taken[RAW[at]] = True
            at += 1
    stream[~taken] = ada[ADA0:]

    mu = a["mu_shift"][0]
    mu27 = np.zeros(27 * 128, f)
    mu27[:2 * LORA + GATE] = mu[low:pooled]
    mu27[384:] = np.concatenate([mu[DR:2 * DR], mu[0:DR], mu[2 * DR:3 * DR]])

    def taps(w, swap):
        t = w.reshape(3, 2, NF, 128)[:, ::-1 if swap else 1]
        return np.ascontiguousarray(t.transpose(3, 2, 1, 0).reshape(128, -1))

    def tiles2(v, swap):
        t = v.reshape(2, NF, 128)[::-1 if swap else 1]
        return np.ascontiguousarray(t.transpose(2, 1, 0).reshape(128, -1))

    named = {
        "c": _columns(a["c"]), "b_ada": _columns(a["b_ada"]), "norm1_g": _columns(a["norm1_g"]), "mu": _columns(mu27),
        "w0": _columns(a["w0"]), "a0": _columns(a["a0"]), "k_k": _columns(a["k_k"]), "k_a": _columns(a["k_a"]),
        "r_k": _columns(a["r_k"]), "ln_w": _columns(a["ln_x_w"]), "ln_b": _columns(a["ln_x_b"]),
        "pool_b": _columns(a["pool_b"]), "pool_scale": _columns(a["pool_scale"]), "norm2_g": _columns(a["norm2_g"]),
        "conv_w": taps(a["conv_w"][0], False), "conv_b": tiles2(a["conv_b"][0], False),
        "norm_f_g": _columns(a["norm_f_g"]), "norm_mix_g": _columns(a["norm_mix_g_2"]), "b_gate": _columns(a["b_gate_2"]),
        "conv_a_w": np.ascontiguousarray(a["conv_a_w_2"][0].reshape(3, NR, 128).transpose(2, 1, 0).reshape(128, -1)),
        "norm_ffn_g": _columns(a["norm_ffn_g_2"]), "conv2_w": taps(a["ffn_conv_w_2"][0], True),
        "conv2_b": tiles2(a["ffn_conv_b_2"][0], True), "norm_final_g": _columns(a["norm_final_g_2"]),
        "sink": np.broadcast_to(a["sink_logits_2"][0][order][None], (128, NQ)),
    }
    params = np.concatenate([named[n] for n, _ in PARAMS], 1)
    lora_w = np.zeros((128, 3, DR), f)
    lora_w[:64, 0], lora_w[64:, 0] = a["w2"][0], a["a2"][0]
    lora_w[:, 1], lora_w[:GATE - 128, 2] = a["g2"][0][:128], a["g2"][0][128:]
    pool_w = a["pool_w"][0].reshape(NPOOL, 2, 128, 2, 128).transpose(2, 0, 1, 3, 4).reshape(128, -1)
    res, wkv, att, inv = _constants()
    x_in = a["x"][0].T.reshape(KT, 128, T).transpose(1, 0, 2)
    arrays = {"stream": stream, "x": x_in, "params": params, "lora": lora_w, "pool_w": pool_w, "pool_inv": inv,
              "res": res, "wkv": wkv, "att": att}
    arrays = {f"in_{k}_dram": np.ascontiguousarray(v) for k, v in arrays.items()}
    nc = _bacc.Bacc("TRN2", target_bir_lowering=False, num_devices=1, dynamic_dma_scratch_size=SCRATCH)
    args = [nc.dram_tensor(k, v.shape, F32, kind="ExternalInput").ap() for k, v in arrays.items()]
    args.append(nc.dram_tensor("out_0_dram", (P, KT, T), F32, kind="ExternalOutput").ap())
    build(nc, args)
    r = _run(nc, [arrays], core_ids=[0])
    y = r.results[0]["out_0_dram"]
    return np.ascontiguousarray(y.transpose(1, 0, 2).reshape(DM, T).T)[None]
```
